# Optimizing a Trainium2 kernel written in Bass

```python
import jax, jax.numpy as jnp
from jax import lax
import numpy as np

D_MODEL = 1024
BATCH = 1
SEQ = 2048
DEPTH = 1

MIX_WIDTH = D_MODEL
RET_HEADS = 8
RET_WIDTH = MIX_WIDTH // 2
RET_V_DIM = RET_WIDTH // RET_HEADS
RET_QK_DIM = RET_V_DIM // 2
RET_CHUNK = 128
RET_ROT_BASE = 10000.0
ATT_HEADS = 8
ATT_WIDTH = MIX_WIDTH - RET_WIDTH
ATT_HEAD_DIM = ATT_WIDTH // ATT_HEADS
DILATED_PATTERNS = ((128, 1), (512, 4), (2048, 16))
ATT_BLOCK = 128
ROPE_THETA = 500000.0
ROPE_DIM = ATT_HEAD_DIM // 4
D_FF = -(-8 * D_MODEL // (3 * 256)) * 256
RMS_EPS = 1e-6
GN_EPS = 1e-5
PROJ_SPLITS = (RET_HEADS * RET_QK_DIM, RET_HEADS * RET_QK_DIM, RET_WIDTH, RET_WIDTH,
               ATT_WIDTH, ATT_WIDTH, ATT_WIDTH)
PROJ_WIDTH = sum(PROJ_SPLITS)

kernel_name = 'hybrid_retention_dilated_attn_block'

def rms_norm(x, g):
    xf = x.astype(jnp.float32)
    y = xf * lax.rsqrt(jnp.mean(xf * xf, axis=-1, keepdims=True) + RMS_EPS)
    return (y * g.astype(jnp.float32)).astype(x.dtype)

def apply_rotary(x, pos, inv_freq):
    rot = 2 * inv_freq.shape[0]
    ang = pos.astype(jnp.float32)[:, :, None] * inv_freq[None, None, :]
    cos = jnp.cos(ang)[:, :, None, :]
    sin = jnp.sin(ang)[:, :, None, :]
    xr = x[..., :rot].astype(jnp.float32)
    x1, x2 = xr[..., :rot // 2], xr[..., rot // 2:]
    out = jnp.concatenate([x1 * cos - x2 * sin, x1 * sin + x2 * cos], axis=-1).astype(x.dtype)
    return jnp.concatenate([out, x[..., rot:]], axis=-1)

def retention_branch(q, k, v, g, pos):
    B, S, H, dk = q.shape
    dv = v.shape[-1]
    inv_freq = 1.0 / (RET_ROT_BASE ** jnp.linspace(0.0, 1.0, dk // 2, dtype=jnp.float32))
    q = apply_rotary(q, pos, inv_freq)
    k = apply_rotary(k, pos, inv_freq) * (dk ** -0.5)
    C = RET_CHUNK
    N = S // C
    log_g = jnp.log1p(-jnp.exp2(-5.0 - jnp.arange(H, dtype=jnp.float32)))
    idx = jnp.arange(C, dtype=jnp.float32)
    diff = idx[:, None] - idx[None, :]
    inner_decay = jnp.where(diff >= 0, jnp.exp(log_g[:, None, None] * jnp.maximum(diff, 0.0)), 0.0)
    q_decay = jnp.exp(log_g[:, None] * (idx + 1.0)[None, :])
    k_decay = jnp.exp(log_g[:, None] * (C - 1.0 - idx)[None, :])
    chunk_decay = jnp.exp(log_g * C)
    qc = q.reshape(B, N, C, H, dk)
    kc = k.reshape(B, N, C, H, dk)
    vc = v.reshape(B, N, C, H, dv)
    scores = jnp.einsum('bnchd,bnmhd->bnhcm', qc, kc) * inner_decay
    inner = jnp.einsum('bnhcm,bnmhe->bnche', scores, vc)
    kv = jnp.einsum('bnchd,hc,bnche->nbhde', kc, k_decay, vc)

    def step(state, kv_i):
        return chunk_decay[None, :, None, None] * state + kv_i, state

    _, prev_states = lax.scan(step, jnp.zeros((B, H, dk, dv), dtype=kv.dtype), kv)
    cross = jnp.einsum('bnchd,nbhde,hc->bnche', qc, prev_states, q_decay)
    out = (inner + cross).reshape(B, S, H, dv).astype(jnp.float32)
    mu = jnp.mean(out, axis=-1, keepdims=True)
    var = jnp.mean(jnp.square(out - mu), axis=-1, keepdims=True)
    out = ((out - mu) * lax.rsqrt(var + GN_EPS)).astype(v.dtype)
    return (out * jax.nn.silu(g)).reshape(B, S, H * dv)

def dilated_pattern(q, k, v, window, dilation):
    B, S, H, D = q.shape
    Lc = S // dilation
    wc = window // dilation
    nb = -(-Lc // ATT_BLOCK)
    Lp = nb * ATT_BLOCK

    def to_classes(t):
        return t.reshape(B, Lc, dilation, H, D).transpose(0, 2, 3, 1, 4)

    qc = jnp.pad(to_classes(q), ((0, 0), (0, 0), (0, 0), (0, Lp - Lc), (0, 0)))
    qb = qc.reshape(B, dilation, H, nb, ATT_BLOCK, D)
    kv_pad = ((0, 0), (0, 0), (0, 0), (ATT_BLOCK, Lp - Lc), (0, 0))
    kb = jnp.pad(to_classes(k), kv_pad).reshape(B, dilation, H, nb + 1, ATT_BLOCK, D)
    vb = jnp.pad(to_classes(v), kv_pad).reshape(B, dilation, H, nb + 1, ATT_BLOCK, D)
    kcat = jnp.concatenate([kb[:, :, :, :-1], kb[:, :, :, 1:]], axis=-2)
    vcat = jnp.concatenate([vb[:, :, :, :-1], vb[:, :, :, 1:]], axis=-2)
    s = jnp.einsum('brhnqd,brhnkd->brhnqk', qb, kcat).astype(jnp.float32) * (D ** -0.5)
    a = jnp.arange(ATT_BLOCK)
    kk = jnp.arange(2 * ATT_BLOCK)
    blk = jnp.arange(nb)
    dist = ATT_BLOCK + a[:, None] - kk[None, :]
    key_idx = blk[:, None] * ATT_BLOCK - ATT_BLOCK + kk[None, :]
    mask = ((dist >= 0) & (dist <= wc))[None, :, :] & (key_idx >= 0)[:, None, :]
    s = jnp.where(mask, s, -jnp.inf)
    m = jnp.max(s, axis=-1, keepdims=True)
    p = jnp.exp(s - m)
    den = jnp.sum(p, axis=-1)
    o = jnp.einsum('brhnqk,brhnkd->brhnqd', p.astype(v.dtype), vcat).astype(jnp.float32) / den[..., None]
    lse = m[..., 0] + jnp.log(den)
    o = o.reshape(B, dilation, H, Lp, D)[:, :, :, :Lc].transpose(0, 3, 1, 2, 4).reshape(B, S, H, D)
    lse = lse.reshape(B, dilation, H, Lp)[:, :, :, :Lc].transpose(0, 3, 1, 2).reshape(B, S, H)
    return o, lse

def dilated_attention_branch(q, k, v, pos):
    B, S, H, D = q.shape
    inv_freq = ROPE_THETA ** (-jnp.arange(0, ROPE_DIM, 2, dtype=jnp.float32) / ROPE_DIM)
    q = apply_rotary(q, pos, inv_freq)
    k = apply_rotary(k, pos, inv_freq)
    outs, lses = [], []
    for window, dilation in DILATED_PATTERNS:
        o, lse = dilated_pattern(q, k, v, window, dilation)
        outs.append(o)
        lses.append(lse)
    w = jax.nn.softmax(jnp.stack(lses, axis=0), axis=0)
    out = jnp.sum(w[..., None] * jnp.stack(outs, axis=0), axis=0)
    return out.astype(v.dtype).reshape(B, S, H * D)

def setup_inputs(seed: int = 0) -> dict:
    key = jax.random.key(seed)
    ks = jax.random.split(key, 12)

    def gain(k):
        return 1.0 + 0.05 * jax.random.normal(k, (DEPTH, D_MODEL), jnp.float32)

    x = jax.random.normal(ks[0], (BATCH, SEQ, D_MODEL), jnp.float32)
    offsets = jax.random.randint(ks[1], (BATCH, 1), 0, 4096, dtype=jnp.int32)
    positions = (jnp.arange(SEQ, dtype=jnp.int32)[None, :] + offsets).astype(jnp.int32)
    w_in = jax.random.normal(ks[2], (DEPTH, D_MODEL, PROJ_WIDTH), jnp.float32) * D_MODEL ** -0.5
    w_out = jax.random.normal(ks[3], (DEPTH, MIX_WIDTH, D_MODEL), jnp.float32) * MIX_WIDTH ** -0.5
    w_gate = jax.random.normal(ks[4], (DEPTH, D_MODEL, D_FF), jnp.float32) * D_MODEL ** -0.5
    w_up = jax.random.normal(ks[5], (DEPTH, D_MODEL, D_FF), jnp.float32) * D_MODEL ** -0.5
    w_down = jax.random.normal(ks[6], (DEPTH, D_FF, D_MODEL), jnp.float32) * D_FF ** -0.5
    return {'x': x, 'positions': positions, 'w_in': w_in, 'w_out': w_out,
            'g_pre_mix': gain(ks[7]), 'g_post_mix': gain(ks[8]),
            'g_pre_ffn': gain(ks[9]), 'g_post_ffn': gain(ks[10]),
            'w_gate': w_gate, 'w_up': w_up, 'w_down': w_down}

def reference(x, positions, w_in, w_out, g_pre_mix, g_post_mix, g_pre_ffn, g_post_ffn, w_gate, w_up, w_down):
    B, S, _ = x.shape
    split_idx = list(np.cumsum(PROJ_SPLITS)[:-1])
    for l in range(DEPTH):
        h = rms_norm(x, g_pre_mix[l])
        proj = h @ w_in[l]
        rq, rk, rv, rg, aq, ak, av = jnp.split(proj, split_idx, axis=-1)
        ret = retention_branch(rq.reshape(B, S, RET_HEADS, RET_QK_DIM),
                               rk.reshape(B, S, RET_HEADS, RET_QK_DIM),
                               rv.reshape(B, S, RET_HEADS, RET_V_DIM),
                               rg.reshape(B, S, RET_HEADS, RET_V_DIM), positions)
        att = dilated_attention_branch(aq.reshape(B, S, ATT_HEADS, ATT_HEAD_DIM),
                                       ak.reshape(B, S, ATT_HEADS, ATT_HEAD_DIM),
                                       av.reshape(B, S, ATT_HEADS, ATT_HEAD_DIM), positions)
        mix = jnp.concatenate([ret, att], axis=-1) @ w_out[l]
        x = x + rms_norm(mix, g_post_mix[l])
        h = rms_norm(x, g_pre_ffn[l])
        f = (jax.nn.silu(h @ w_gate[l]) * (h @ w_up[l])) @ w_down[l]
        x = x + rms_norm(f, g_post_ffn[l])
    return x


_drawn_inputs = setup_inputs


def setup_inputs(seed=0):
    import zlib

    import numpy as np

    out = dict(_drawn_inputs(seed))
    spreads = {}
    factors = {}
    for name, (base, spread) in spreads.items():
        noise = np.random.default_rng([zlib.crc32(name.encode()), seed]).standard_normal(out[name].shape)
        drawn = base * np.exp(spread * noise) if base else spread * noise
        out[name] = __import__('jax').numpy.asarray(drawn.astype(out[name].dtype))
    for name, factor in factors.items():
        out[name] = (out[name] * factor).astype(out[name].dtype)
    return out
```

```python
import math
from contextlib import ExitStack

import concourse.bass as bass
from concourse import mybir

F32 = mybir.dt.float32
F32R = mybir.dt.float32r
I32 = mybir.dt.int32
ACT = mybir.ActivationFunctionType
ALU = mybir.AluOpType
AX = mybir.AxisListType

P = 128
SEQ = 2048
DM = 1024
KT = DM // P
CHUNKS = SEQ // P
GROUP = 512
GROUPS = SEQ // GROUP
RET_HEADS, RET_DK, RET_DV = 8, 32, 64
ATT_HEADS, ATT_D = 8, 64
RET_QK = RET_HEADS * RET_DK
WIDTH = RET_HEADS * RET_DV
PROJ = 2 * RET_QK + 5 * WIDTH
RQ, RK, RV, RG = 0, RET_QK, 2 * RET_QK, 2 * RET_QK + WIDTH
AQ = RG + WIDTH
AK, AV = AQ + WIDTH, AQ + 2 * WIDTH
ROPE = ATT_D // 4
D_FF = 2816
PATTERNS = (1, 4, 16)
RMS_EPS, GN_EPS = 1e-6, 1e-5
NEG = -1e30
AO_W = 2 * ATT_D + 4


class Mem:

    def __init__(self, nc, ctx, phase):
        self.nc, self.ctx, self.phase = nc, ctx, phase

    def sb(self, name, shape, dt=F32):
        return self.ctx.enter_context(self.nc.sbuf_tensor(f"{self.phase}_{name}", shape, dt))

    def ps(self, name, shape, dt=F32):
        return self.ctx.enter_context(self.nc.psum_tensor(f"{self.phase}_psum_{name}", shape, dt))

    def sem(self, name):
        return self.nc.alloc_semaphore(f"{self.phase}_{name}")

    def sems(self, name, n):
        return [self.sem(f"{name}{i}") for i in range(n)]


def normed_transpose(nc, D, keep):
    hT_hi, hT_lo = keep["hT_hi"], keep["hT_lo"]
    with ExitStack() as ctx:
        m = Mem(nc, ctx, "nt")
        ident = m.sb("ident", [P, P])
        gain = m.sb("gain", [P, DM])
        minus_half = m.sb("minus_half", [P, 1])
        xin = m.sb("xin", [P, 2, DM])
        xn = m.sb("xn", [P, 2, DM])
        squares = m.sb("squares", [P, 2, DM])
        sumsq = m.sb("sumsq", [P, 2])
        meansq = m.sb("meansq", [P, 2])
        rstd = m.sb("rstd", [P, 2])
        tp = m.ps("tp", [P, 2, KT, P])
        consts = m.sem("consts")
        half_set = m.sem("half_set")
        loaded, x_free = m.sems("loaded", 2), m.sem("x_free")
        summed, meaned, rooted, normed = m.sem("summed"), m.sem("meaned"), m.sem("rooted"), m.sem("normed")
        transposed, hi_done, lo_done = m.sem("transposed"), m.sem("hi_done"), m.sem("lo_done")
        with nc.Block() as block:

            @block.sync
            def _(sp):
                sp.dma_start(ident[:], D["ident"]).then_inc(consts, 16)
                sp.dma_start(gain[:], D["g_pre_mix"].broadcast_to([P, DM])).then_inc(consts, 16)
                sp.sem_inc(x_free, 2)
                with sp.Fori(0, CHUNKS // 2) as it:
                    for s in range(2):
                        sp.wait_ge(x_free, 2 * it + s + 1)
                        sp.dma_start(xin[:, s, :], D["x"][bass.ts(2 * it + s, P), :]).then_inc(loaded[s], 16)

            @block.scalar
            def _(act):
                with act.Fori(0, CHUNKS // 2) as it:
                    for s in range(2):
                        act.wait_ge(loaded[s], 16 * it + 16)
                        nc.scalar.activation(squares[:, s, :], xin[:, s, :], ACT.Square,
                                             accum_out=sumsq[:, s:s + 1]).then_inc(summed, 1)
                    for s in range(2):
                        act.wait_ge(transposed, 2 * it + s + 1)
                        nc.scalar.activation(hT_hi[:, :, bass.ts(2 * it + s, P)], tp[:, s], ACT.Copy).then_inc(hi_done, 1)

            @block.gpsimd
            def _(pool):
                nc.gpsimd.memset(minus_half[:], -0.5).then_inc(half_set, 1)
                pool.wait_ge(half_set, 1)
                with pool.Fori(0, CHUNKS // 2) as it:
                    for s in range(2):
                        pool.wait_ge(meaned, 2 * it + s + 1)
                        nc.gpsimd.tensor_tensor(rstd[:, s:s + 1], meansq[:, s:s + 1], minus_half[:],
                                                ALU.pow).then_inc(rooted, 1)

            @block.vector
            def _(dve):
                dve.wait_ge(consts, 32)
                with dve.Fori(0, CHUNKS // 2) as it:
                    for s in range(2):
                        dve.wait_ge(summed, 2 * it + s + 1)
                        nc.vector.tensor_scalar(meansq[:, s:s + 1], sumsq[:, s:s + 1], 1.0 / DM, RMS_EPS,
                                                ALU.mult, ALU.add).then_inc(meaned, 1)
                    for s in range(2):
                        dve.wait_ge(rooted, 2 * it + s + 1)
                        nc.vector.scalar_tensor_tensor(xn[:, s, :], xin[:, s, :], rstd[:, s:s + 1], gain[:],
                                                       ALU.mult, ALU.mult).then_inc(normed, 1)
                        dve.wait_ge(normed, 2 * it + s + 1)
                        dve.sem_inc(x_free, 1)
                    for s in range(2):
                        dve.wait_ge(hi_done, 2 * it + s + 1)
                        nc.vector.tensor_tensor(hT_lo[:, :, bass.ts(2 * it + s, P)], tp[:, s],
                                                hT_hi[:, :, bass.ts(2 * it + s, P)].bitcast(F32),
                                                ALU.subtract).then_inc(lo_done, 1)

            @block.tensor
            def _(pe):
                pe.sem_inc(lo_done, 2)
                pe.wait_ge(consts, 32)
                with pe.Fori(0, CHUNKS // 2) as it:
                    for s in range(2):
                        pe.wait_ge(normed, 2 * it + s + 1)
                        pe.wait_ge(lo_done, 2 * it + s + 1)
                        for k in range(KT):
                            last = nc.tensor.transpose(tp[:, s, k, :], xn[:, s, k * P:(k + 1) * P], ident[:])
                        last.then_inc(transposed, 1)


def turns_parts():
    left, parts = 2 * math.pi, []
    for _ in range(3):
        unit = 2.0 ** (math.floor(math.log2(left)) - 7)
        parts.append(math.floor(left / unit) * unit)
        left -= parts[-1]
    return parts + [left]


SECTIONS = ((RV // 256, 2, "copy"), (RG // 256, 2, "silu"), (RQ // 256, 2, "ret"), (AQ // 256, 4, "att"),
            (AV // 256, 2, "copy"))


def project(nc, D, keep):
    hT_hi, hT_lo = keep["hT_hi"], keep["hT_lo"]
    pairs = PROJ // (2 * P)
    NR = 4
    C_ADDED = 2
    SWAP = {"ret": [(i + RET_DK // 2) % RET_DK for i in range(RET_DK)],
            "att": [(i + ROPE // 2) % ROPE if i < ROPE else i for i in range(32)]}
    with ExitStack() as ctx:
        m = Mem(nc, ctx, "pr")
        raw = m.sb("raw", [P, KT, P])
        w_hi = m.sb("w_hi", [P, 2, KT, P], F32R)
        w_lo = m.sb("w_lo", [P, 2, KT, P], F32R)
        rows = m.sb("rows", [P, NR, GROUP])
        swap = m.sb("swap", [P, 2, GROUP])
        hi = m.sb("hi", [P, 2, GROUP], F32R)
        lo = m.sb("lo", [P, 2, GROUP], F32R)
        rotation = m.sb("rotation", [P, 4])
        quarter = m.sb("quarter", [P, 1])
        part = m.sb("part", [P, SEQ // 2])
        table = {kind: (m.sb(f"cos_{kind}", [P, SEQ]), m.sb(f"sin_{kind}", [P, SEQ])) for kind in ("ret", "att")}
        acc = m.ps("acc", [P, 2, GROUPS, GROUP])
        w_loaded, split = m.sem("w_loaded"), m.sem("split")
        hi_split = m.sem("hi_split")
        tile_done = m.sem("tile_done")
        group_done = m.sem("group_done")
        copied = m.sem("copied")
        row_free = m.sems("row_free", NR)
        shuffled, scaled, added, hi_done, lo_done = m.sem("shuffled"), m.sem("scaled"), m.sem("added"), m.sem("hi_done"), m.sem("lo_done")
        scaled0 = m.sem("scaled0")
        waited = m.sem("waited")
        parts_stored = m.sems("parts_stored", 2)
        consts, angle_step, tables_done = m.sem("consts"), m.sem("angle_step"), m.sem("tables_done")
        angles = m.sems("angles", 2)

        def sections():
            pos = 0
            for first, n, kind in SECTIONS:
                yield kind, first, first + n, pos - first
                pos += n

        ROT0 = 4
        ATT0 = 6

        with nc.Block() as block:

            @block.sync
            def _(sp):
                sp.dma_start(rotation[:], D["rotation"]).then_inc(consts, 16)
                for kind in ("ret", "att"):
                    sp.dma_start(table[kind][1][:].bitcast(I32), D["positions"].broadcast_to([P, SEQ])).then_inc(consts, 16)

                def load(column):
                    sp.dma_start(raw[:], D["w_in"][:, bass.ds(column, P)].rearrange("(k p) n -> p k n", p=P)).then_inc(w_loaded, 16)

                tiles = [2 * pair + s for first, n, _ in SECTIONS for pair in range(first, first + n) for s in range(2)]
                load(tiles[0] * P)
                sp.wait_ge(split, 1)
                load(tiles[1] * P)
                flat = list(sections())
                for n, (kind, first, end, shift) in enumerate(flat):
                    def body(pair, following):
                        pos = pair + shift
                        for s in range(2):
                            for g in range(GROUPS):
                                t = slice(g * GROUP, (g + 1) * GROUP)
                                at = bass.ds(pair * 2 * P + s * P, P)
                                i = s * GROUPS + g
                                if kind == "att":
                                    a = 8 * (pos - ATT0) + i
                                    sp.wait_ge(lo_done, a + 1)
                                    to = bass.ds(pair * 2 * P + s * P - AQ, P)
                                    sp.dma_start(D["rot_hi"][to, t], hi[:, i % 2, :].bitcast(F32)).then_inc(parts_stored[i % 2], 16)
                                    sp.dma_start(D["rot_lo"][to, t], lo[:, i % 2, :].bitcast(F32)).then_inc(parts_stored[i % 2], 16)
                                else:
                                    if kind == "ret":
                                        sp.wait_ge(added, 8 * (pos - ROT0) + i + 1 + C_ADDED)
                                    else:
                                        sp.wait_ge(copied, 8 * pos + i + 1 + 8)
                                    sp.dma_start(D["projT"][at, t], rows[:, i % NR, :]).then_inc(row_free[i % NR], 16)
                            if following is not None:
                                sp.wait_ge(split, 2 * pos + s + 2)
                                load(following * 2 * P + s * P)

                    if end - first > 1:
                        with sp.Fori(first, end - 1) as pair:
                            body(pair, pair + 1)
                    body(end - 1, flat[n + 1][1] if n + 1 < len(flat) else None)
                for r in range(NR):
                    sp.wait_ge(row_free[r], 16 * (8 * pairs // NR) + 16)
                for r in range(2):
                    sp.wait_ge(parts_stored[r], 32 * 16 + 32)

            @block.vector
            def _(dve):
                dve.sem_inc(tile_done, 2)
                dve.wait_ge(consts, 48)
                pi = 3.1415925

                def split_tile(pos, s):
                    t = 2 * pos + s
                    dve.wait_ge(w_loaded, 16 * t + 16)
                    dve.wait_ge(tile_done, t + 1)
                    nc.vector.tensor_copy(w_hi[:, s], raw[:]).then_inc(hi_split, 1)
                    dve.wait_ge(hi_split, t + 1)
                    nc.vector.tensor_tensor(w_lo[:, s], raw[:], w_hi[:, s].bitcast(F32), ALU.subtract).then_inc(split, 1)

                split_tile(0, 0)
                split_tile(0, 1)

                def shuffle(kind, pos, i):
                    q = 8 * (pos - ROT0) + i
                    dve.wait_ge(copied, 8 * pos + i + 1 + 8)
                    dve.wait_ge(added, q + 1 - 2 + C_ADDED)
                    dve.sem_inc(waited, 1)
                    nc.vector.stream_shuffle(swap[:, i % 2, :], rows[:, i % NR, :], SWAP[kind]).then_inc(shuffled, 1)

                def add(pos, i):
                    q = 8 * (pos - ROT0) + i
                    dve.wait_ge(scaled, q + 1)
                    nc.vector.tensor_tensor(rows[:, i % NR, :], rows[:, i % NR, :], swap[:, i % 2, :], ALU.add).then_inc(added, 1)

                def lows(pos, i):
                    a = 8 * (pos - ATT0) + i
                    dve.wait_ge(hi_done, a + 1)
                    nc.vector.tensor_tensor(lo[:, i % 2, :], rows[:, i % NR, :], hi[:, i % 2, :].bitcast(F32), ALU.subtract).then_inc(lo_done, 1)
                    dve.wait_ge(lo_done, a + 1)
                    dve.sem_inc(row_free[i % NR], 16)

                for kind, first, end, shift in sections():
                    rotated = kind in ("ret", "att")

                    def body(pair):
                        pos = pair + shift
                        for s in range(2):
                            if rotated:
                                for g in range(GROUPS):
                                    i = s * GROUPS + g
                                    shuffle(kind, pos, i)
                                    if g:
                                        add(pos, i - 1)
                                    if g > 1 and kind == "att":
                                        lows(pos, i - 2)
                                add(pos, i)
                                if kind == "att":
                                    lows(pos, i - 1)
                                    lows(pos, i)
                            split_tile(pos + 1, s)

                    closing = shift + end == pairs
                    with dve.Fori(first, end - 1 if closing else end) as pair:
                        body(pair)

            @block.tensor
            def _(pe):
                pe.sem_inc(copied, 2 * GROUPS)
                with pe.Fori(0, pairs) as pos:
                    for s in range(2):
                        pe.wait_ge(split, 2 * pos + s + 1)
                        for g in range(GROUPS):
                            pe.wait_ge(copied, 8 * pos + s * GROUPS + g + 1)
                            t = slice(g * GROUP, (g + 1) * GROUP)
                            n = 0
                            for k in range(KT):
                                for w, h in ((w_hi, hT_hi), (w_hi, hT_lo), (w_lo, hT_hi)):
                                    last = nc.tensor.matmul(acc[:, s, g, :], w[:, s, k, :], h[:, k, t],
                                                            start=n == 0, stop=n == 3 * KT - 1)
                                    n += 1
                            last.then_inc(group_done, 1)
                        pe.wait_ge(group_done, 8 * pos + (s + 1) * GROUPS)
                        pe.sem_inc(tile_done, 1)

            @block.scalar
            def _(act):
                for r in range(NR):
                    act.sem_inc(row_free[r], 16)
                for r in range(2):
                    act.sem_inc(parts_stored[r], 32)
                act.sem_inc(added, C_ADDED)
                for kind, first, end, shift in sections():
                    if kind == "ret":
                        for n, (of, c) in enumerate((("ret", 2), ("att", 0))):
                            cosT, sinT = table[of]
                            act.wait_ge(angles[n], 1)
                            nc.scalar.activation(sinT[:], cosT[:], ACT.Sin, scale=rotation[:, c + 1:c + 2]).then_inc(tables_done, 1)
                            act.wait_ge(tables_done, 3 * n + 1)
                            nc.scalar.activation(cosT[:], cosT[:], ACT.Abs).then_inc(tables_done, 1)
                            act.wait_ge(tables_done, 3 * n + 2)
                            nc.scalar.activation(cosT[:], cosT[:], ACT.Sin, bias=quarter[:], scale=-1.0).then_inc(tables_done, 1)

                    def high(pos, i):
                        a = 8 * (pos - ATT0) + i
                        act.wait_ge(added, a + 8 * (ATT0 - ROT0) + 1 + C_ADDED)
                        act.wait_ge(parts_stored[i % 2], 32 * 4 * (pos - ATT0) + 32 * (i // 2) + 32)
                        nc.scalar.activation(hi[:, i % 2, :], rows[:, i % NR, :], ACT.Copy).then_inc(hi_done, 1)

                    with act.Fori(first, end) as pair:
                        pos = pair + shift
                        for i in range(8):
                            act.wait_ge(row_free[i % NR], 32 * pos + 16 * (i // NR) + 16)
                            act.wait_ge(group_done, 8 * pos + i + 1)
                            nc.scalar.activation(rows[:, i % NR, :], acc[:, i // GROUPS, i % GROUPS, :],
                                                 ACT.Silu if kind == "silu" else ACT.Copy).then_inc(copied, 1)
                            if kind == "att" and i % GROUPS:
                                high(pos, i - 1)
                            if kind == "att" and i % GROUPS == GROUPS - 1:
                                high(pos, i)

            @block.gpsimd
            def _(pool):
                step = [0]

                def then(instruction):
                    step[0] += 1
                    instruction.then_inc(angle_step, 1)
                    pool.wait_ge(angle_step, step[0])

                MAGIC = 1.5 * 2.0 ** 23
                pool.wait_ge(consts, 48)
                then(nc.gpsimd.memset(quarter[:], math.pi / 2))
                for n, (kind, c) in enumerate((("ret", 2), ("att", 0))):
                    angle, turns = table[kind]
                    then(nc.gpsimd.tensor_copy(angle[:], turns[:].bitcast(I32)))
                    then(nc.gpsimd.tensor_scalar(angle[:], angle[:], rotation[:, c:c + 1], None, ALU.mult))
                    then(nc.gpsimd.tensor_scalar(turns[:], angle[:], 1 / (2 * math.pi), MAGIC, ALU.mult, ALU.add))
                    then(nc.gpsimd.tensor_scalar(turns[:], turns[:], -MAGIC, None, ALU.add))
                    for half in range(2):
                        h = slice(half * SEQ // 2, (half + 1) * SEQ // 2)
                        for value in turns_parts():
                            then(nc.gpsimd.tensor_scalar(part[:], turns[:, h], value, None, ALU.mult))
                            then(nc.gpsimd.tensor_tensor(angle[:, h], angle[:, h], part[:], ALU.subtract))
                    then(nc.gpsimd.tensor_scalar(angle[:], angle[:], 3.1415925, -3.1415925, ALU.min, ALU.max))
                    pool.sem_inc(angles[n], 1)
                pool.wait_ge(tables_done, 6)
                for kind, first, end, shift in sections():
                    if kind not in ("ret", "att"):
                        continue
                    cosT, sinT = table[kind]
                    with pool.Fori(first, end) as pair:
                        for i in range(8):
                            q = 8 * (pair + shift - ROT0) + i
                            t = slice(i % GROUPS * GROUP, (i % GROUPS + 1) * GROUP)
                            pool.wait_ge(shuffled, q + 1)
                            nc.gpsimd.tensor_tensor(swap[:, i % 2, :], swap[:, i % 2, :], sinT[:, t], ALU.mult).then_inc(scaled0, 1)
                            pool.wait_ge(scaled0, q + 1)
                            nc.gpsimd.tensor_tensor(rows[:, i % NR, :], rows[:, i % NR, :], cosT[:, t], ALU.mult).then_inc(scaled, 1)


def attention_blocks():
    out = []
    for p, d in enumerate(PATTERNS):
        for r in range(d):
            for n in range(CHUNKS // d):
                out.append((p, r + d * P * n, d, n > 0))
    return out


def attention(nc, D):
    blocks = attention_blocks()
    NB = len(blocks)
    NU = ATT_HEADS // 2
    NV = NB // 4
    SCALE = ATT_D ** -0.5
    RING = 8
    with ExitStack() as ctx:
        m = Mem(nc, ctx, "at")
        ident = m.sb("ident", [P, P])
        mask = m.sb("mask", [P, 2 * P])
        q2 = m.sb("q2", [P, 2, 2, SEQ], F32R)
        k_hi2 = m.sb("k_hi2", [P, 2, 2, SEQ], F32R)
        k_lo2 = m.sb("k_lo2", [P, 2, 2, SEQ], F32R)
        vT = m.sb("vT", [P, SEQ])
        vblk = m.sb("vblk", [P, NB, P])
        prob = m.sb("prob", [P, 4, 2, 2 * P])
        probT = m.sb("probT", [P, 2, 2, 2, P])
        bias = m.sb("bias", [P, 4, 2])
        orow = m.sb("orow", [P, RING, AO_W])
        s_ps = m.ps("s", [P, 2, 2, 512])
        t_ps = m.ps("t", [P, 2, 2, 2, P])
        o_ps = m.ps("o", [P, 2, 2 * P])
        v_ps = m.ps("v", [P, 4, P])
        consts = m.sem("consts")
        qk_loaded, v_loaded = m.sems("qk_loaded", 2), m.sem("v_loaded")
        scored, maxed, biased, exped = m.sem("scored"), m.sem("maxed"), m.sem("biased"), m.sem("exped")
        turned = m.sem("turned")
        turn_copied = m.sems("turn_copied", 2)
        valued, o_copied = m.sem("valued"), m.sem("o_copied")
        waited = m.sem("waited")
        v_turned, v_copied = m.sem("v_turned"), m.sem("v_copied")
        stored = m.sems("stored", RING)
        C_MAXED, C_TURNED, C_COPIED, C_VALUED, C_O, C_V = 2, 4, 1, 2, 1, 1
        C_SCORED = 1
        keys = [slice(0, 2 * P) if b[3] else slice(P, 2 * P) for b in blocks]
        QK_DMAS = 12

        with nc.Block() as block:

            @block.sync
            def _(sp):
                sp.dma_start(ident[:], D["ident"]).then_inc(consts, 16)
                sp.dma_start(mask[:], D["mask"]).then_inc(consts, 16)

                def load_qk(u, s):
                    for h in range(2):
                        q, k = bass.ds(u * P + h * ATT_D, ATT_D), bass.ds(WIDTH + u * P + h * ATT_D, ATT_D)
                        for tile, upper, lower, rows in ((q2, "rot_hi", "rot_lo", q), (k_hi2, "rot_hi", "rot_hi", k),
                                                         (k_lo2, "rot_lo", "rot_lo", k)):
                            for at, part in ((0, upper), (ATT_D, lower)):
                                sp.dma_start(tile[at:at + ATT_D, s, h, :].bitcast(F32), D[part][rows, :]).then_inc(qk_loaded[s], 16)

                def load_v(u):
                    sp.dma_start(vT[:], D["projT"][AV:AV + WIDTH, :][bass.ts(u, P), :]).then_inc(v_loaded, 16)

                def store(u, j):
                    p, t0, d, _ = blocks[j]
                    sp.wait_ge(o_copied, NB * u + j + 1 + C_O)
                    dst = D["att_out"][p, t0:t0 + d * (P - 1) + 1:d, :]
                    sp.dma_start(dst[:, bass.ds(u * AO_W, AO_W)], orow[:, j % RING, :]).then_inc(stored[j % RING], 16)

                def unit(u, s, more=True):
                    if more:
                        sp.wait_ge(scored, NB * u + C_SCORED)
                        load_qk(u + 1, 1 - s)
                    for j in range(NB):
                        if more and j == NB - 6:
                            sp.wait_ge(v_turned, NV * u + NV)
                            load_v(u + 1)
                        store(u, j)

                load_qk(0, 0)
                load_v(0)
                with sp.Fori(0, NU // 2 - 1) as it:
                    unit(2 * it, 0)
                    unit(2 * it + 1, 1)
                unit(NU - 2, 0)
                unit(NU - 1, 1, more=False)
                for r in range(RING):
                    sp.wait_ge(stored[r], 16 * (NU * NB // RING) + 16)

            @block.tensor
            def _(pe):
                pe.sem_inc(scored, C_SCORED)
                pe.wait_ge(consts, 32)

                def transpose_values(g, u, gi):
                    if gi == 0:
                        pe.wait_ge(v_loaded, 16 * u + 16)
                    pe.wait_ge(v_copied, NV * u + gi + 1)
                    for b in range(4):
                        _, t0, d, _ = blocks[4 * gi + b]
                        last = nc.tensor.transpose(v_ps[:, b, :], vT[:, t0:t0 + d * (P - 1) + 1:d], ident[:])
                    last.then_inc(v_turned, 1)

                def scores(it, u, s, j):
                    _, t0, d, before = blocks[j]
                    k0 = t0 - d * P if before else t0
                    nk = 2 * P if before else P
                    if j == 0:
                        pe.wait_ge(qk_loaded[s], 16 * QK_DMAS * it + 16 * QK_DMAS)
                    pe.wait_ge(maxed, NB * u + j + 1)
                    for h in range(2):
                        q = q2[:, s, h, t0:t0 + d * (P - 1) + 1:d]
                        for k in (k_hi2, k_lo2):
                            last = nc.tensor.matmul(s_ps[:, j % 2, h, keys[j]], q, k[:, s, h, k0:k0 + d * (nk - 1) + 1:d],
                                                    start=k is k_hi2, stop=k is k_lo2)
                    last.then_inc(scored, 1)

                def turn(u, j):
                    pe.wait_ge(exped, NB * u + j + 1)
                    pe.wait_ge(turn_copied[j % 2], (NB // 2) * u + j // 2 + 1)
                    for h in range(2):
                        for kb in range(2):
                            if kb == 1 or blocks[j][3]:
                                last = nc.tensor.transpose(t_ps[:, j % 2, h, kb, :], prob[:, j % 4, h, kb * P:(kb + 1) * P], ident[:])
                    last.then_inc(turned, 1)

                def values(u, j):
                    if j % 4 == 0:
                        pe.wait_ge(v_copied, NV * u + j // 4 + 1 + C_V)
                    pe.wait_ge(turn_copied[j % 2], (NB // 2) * u + j // 2 + 1 + C_COPIED)
                    pe.wait_ge(o_copied, NB * u + j + 1)
                    first = 0 if blocks[j][3] else 1
                    for h in range(2):
                        out = o_ps[:].rearrange("p a b -> p (a b)")[:, h * (2 * P - ATT_D):h * (2 * P - ATT_D) + P]
                        for kb in range(first, 2):
                            last = nc.tensor.matmul(out, probT[:, j % 2, h, kb, :], vblk[:, j - 1 + kb, :],
                                                    start=kb == first, stop=kb == 1)
                    last.then_inc(valued, 1)

                with pe.Fori(0, NU // 2) as it:
                    def at(J):
                        return 2 * it + J // NB, J // NB, J % NB

                    transpose_values(0, 2 * it, 0)
                    for J in range(3):
                        scores(it, *at(J))
                    turn(2 * it, 0)
                    for J in range(2 * NB):
                        u, s, j = at(J)
                        if j % 4 == 0 and j // 4 + 1 < NV:
                            transpose_values(0, u, j // 4 + 1)
                        if J == NB - 1:
                            transpose_values(0, u + 1, 0)
                        if j == NB - 1:
                            values(u, j)
                        if J + 3 < 2 * NB:
                            scores(it, *at(J + 3))
                        if J + 1 < 2 * NB:
                            un, _, jn = at(J + 1)
                            turn(un, jn)
                        if j < NB - 1:
                            values(u, j)

            @block.vector
            def _(dve):
                dve.sem_inc(maxed, C_MAXED)
                dve.sem_inc(turn_copied[0], C_COPIED)
                dve.sem_inc(v_copied, C_V)
                dve.sem_inc(turned, C_TURNED)
                for r in range(RING):
                    dve.sem_inc(stored[r], 16)
                dve.wait_ge(consts, 32)

                def copy_values(u, gi):
                    dve.wait_ge(v_turned, NV * u + gi + 1)
                    nc.vector.tensor_copy(vblk[:, 4 * gi:4 * gi + 4, :], v_ps[:]).then_inc(v_copied, 1)

                def copy_turned(u, j):
                    dve.wait_ge(valued, NB * u + j + 1)
                    dve.wait_ge(turned, NB * u + j + 1 + C_TURNED)
                    kb = 0 if blocks[j][3] else 1
                    nc.vector.tensor_copy(probT[:, 0, :, kb:, :], t_ps[:, 0, :, kb:, :]).then_inc(turn_copied[0], 1)

                with dve.Fori(0, NU) as u:
                    copy_values(u, 0)
                    for j in range(NB):
                        dve.wait_ge(scored, NB * u + j + 1 + C_SCORED)
                        dve.wait_ge(turned, NB * u + j + 1)
                        dve.wait_ge(stored[j % RING], 16 * (NB // RING) * u + 16 * (j // RING) + 16)
                        dve.sem_inc(waited, 1)
                        for h in range(2):
                            last = nc.vector.tensor_tensor_reduce(
                                out=prob[:, j % 4, h, keys[j]], in0=s_ps[:, j % 2, h, keys[j]], in1=mask[:, keys[j]],
                                scale=1.0, scalar=3 * NEG, op0=ALU.add, op1=ALU.max,
                                accum_out=orow[:, j % RING, 2 * ATT_D + h:2 * ATT_D + h + 1])
                        last.then_inc(maxed, 1)
                        dve.wait_ge(maxed, NB * u + j + 1 + C_MAXED)
                        nc.vector.tensor_scalar(bias[:, j % 4, :], orow[:, j % RING, 2 * ATT_D:2 * ATT_D + 2], -SCALE, None,
                                                ALU.mult).then_inc(biased, 1)
                        if j >= 2 and j % 2 == 0:
                            copy_turned(u, j - 2)
                        if j >= 3 and (j - 3) % 4 == 0 and (j - 3) // 4 + 1 < NV:
                            copy_values(u, (j - 3) // 4 + 1)
                    copy_turned(u, NB - 2)

            @block.gpsimd
            def _(pool):
                pass

            @block.scalar
            def _(act):
                act.sem_inc(turn_copied[1], C_COPIED)
                act.sem_inc(valued, C_VALUED)
                act.sem_inc(o_copied, C_O)

                def copy_turned(u, j):
                    act.wait_ge(valued, NB * u + j + 1)
                    act.wait_ge(turned, NB * u + j + 1 + C_TURNED)
                    kb = 0 if blocks[j][3] else 1
                    nc.scalar.activation(probT[:, 1, :, kb:, :], t_ps[:, 1, :, kb:, :], ACT.Copy).then_inc(turn_copied[1], 1)

                def copy_out(u, j):
                    act.wait_ge(valued, NB * u + j + 1 + C_VALUED)
                    nc.scalar.activation(orow[:, j % RING, 0:2 * ATT_D].rearrange("p (h c) -> p h c", h=2), o_ps[:, :, 0:ATT_D], ACT.Copy).then_inc(o_copied, 1)

                with act.Fori(0, NU) as u:
                    for j in range(NB):
                        act.wait_ge(biased, NB * u + j + 1)
                        for h in range(2):
                            pr = prob[:, j % 4, h, keys[j]]
                            last = nc.scalar.activation(pr, pr, ACT.Exp, bias=bias[:, j % 4, h:h + 1], scale=SCALE,
                                                        accum_out=orow[:, j % RING, 2 * ATT_D + 2 + h:2 * ATT_D + 3 + h])
                        last.then_inc(exped, 1)
                        if j >= 2 and j % 2 == 1:
                            copy_turned(u, j - 2)
                        if j >= 3:
                            copy_out(u, j - 3)
                    copy_turned(u, NB - 1)
                    for j in range(NB - 3, NB):
                        copy_out(u, j)


def mix(nc, D):
    NU = 2
    HU = RET_HEADS // NU
    SCALE = ATT_D ** -0.5
    QW = ATT_HEADS // 2 * AO_W
    with ExitStack() as ctx:
        m = Mem(nc, ctx, "mx")
        w_hi = m.sb("w_hi", [P, KT, DM], F32R)
        w_lo = m.sb("w_lo", [P, KT, DM], F32R)
        ident = m.sb("ident", [P, P])
        k_decay = m.sb("k_decay", [P, NU, P])
        q_decay = m.sb("q_decay", [P, NU, P])
        decay = m.sb("decay", [P, NU, HU, P])
        head_rows = m.sb("head_rows", [P, HU])
        head_cols = m.sb("head_cols", [P, HU * RET_DV])
        chunk_decay = m.sb("chunk_decay", [P, NU])
        gain_mix = m.sb("gain_mix", [P, DM])
        gain_ffn = m.sb("gain_ffn", [P, DM])
        minus_half = m.sb("minus_half", [P, RET_HEADS])
        qkv = m.sb("qkv", [P, 2, 8, P])
        q_heads = m.sb("q_heads", [P, NU, HU, P])
        q_dec = m.sb("q_dec", [P, NU, P])
        k_dec = m.sb("k_dec", [P, NU, P])
        v_pad = m.sb("v_pad", [P, 2, RET_HEADS, P])
        probT = m.sb("probT", [P, NU, HU, P])
        kv = m.sb("kv", [P, NU, HU * RET_DV])
        state = m.sb("state", [P, 2, NU, HU * RET_DV])
        stat = m.sb("stat", [P, 4, RET_HEADS])
        centred = m.sb("centred", [P, RET_HEADS, RET_DV])
        squares = m.sb("squares", [P, RET_HEADS, RET_DV])
        row_squares = m.sb("row_squares", [P, 2, DM])
        ret = m.sb("ret", [P, WIDTH])
        att_in = m.sb("att_in", [P, 2, 3, QW])
        gate = m.sb("gate", [P, 2, 4, P])
        att_max = m.sb("att_max", [P, 8])
        weight = m.sb("weight", [P, 3, 8])
        scaled_sum = m.sb("scaled_sum", [P, 3, 8])
        sum8 = m.sb("sum8", [P, 8])
        parts = m.sb("parts", [P, 3, 8, ATT_D])
        mixT = m.sb("mixT", [P, 4, P])
        mT_hi = m.sb("mT_hi", [P, 2, KT, P], F32R)
        mT_lo = m.sb("mT_lo", [P, 2, KT, P], F32R)
        xin = m.sb("xin", [P, DM])
        x1 = m.sb("x1", [P, DM])
        h2 = m.sb("h2", [P, DM])
        ssq = m.sb("ssq", [P, 4])
        hT_hi = m.sb("hT_hi", [P, KT, P], F32R)
        hT_lo = m.sb("hT_lo", [P, KT, P], F32R)
        tp = m.ps("tp", [P, KT, P])
        s_ps = m.ps("s", [P, NU, HU, P])
        o_ps = m.ps("o", [P, RET_HEADS, RET_DV])
        kv_ps = m.ps("kv", [P, NU, HU * RET_DV])
        y_ps = m.ps("y", [P, 2, GROUP])

        names = ("waited consts w_loaded w_split w_hi_split zeroed turned k_done v_done q_ready q_dec_ready "
                 "scored prob_done output kv_done kv_masked state_done summed meaned centre_done squared var_sum var_done "
                 "rooted ret_done maxed differed exped dens_done sum_done recip_done weighted parted parts_a att_done "
                 "mix_turned gated hi_a hi_b lo_a lo_b y_done y_sq y_mean y_root y_scaled x1_done half_set x_sq x_mean x_root "
                 "h2_done h_turned h_hi h_lo").split()
        S = {n: m.sem(n) for n in names}
        qkv_loaded, att_loaded = m.sems("qkv_loaded", 2), m.sems("att_loaded", 2)
        x_loaded, x1_stored, h_stored = m.sem("x_loaded"), m.sem("x1_stored"), m.sem("h_stored")
        CONSTS = 9
        w_raw = parts[:].rearrange("p a h d -> p (a h d)")[:, 0:DM]

        LAG_MIX, LAG_OUT, LAG_H = 1, 2, 3
        FIRST, LAST = LAG_H + 1, CHUNKS - 2

        def steps(eng, step):
            for c in range(FIRST):
                step(c, c % 2, lambda lag, c=c: c - lag >= 0)
            with eng.Fori(0, (LAST - FIRST) // 2) as it:
                for s in range(2):
                    step(2 * it + (FIRST + s), s, lambda lag: True)
            for c in range(LAST, CHUNKS + LAG_H):
                step(c, c % 2, lambda lag, c=c: c - lag < CHUNKS)

        with nc.Block() as block:

            @block.sync
            def _(sp):
                def taken():
                    sp.sem_inc(S["waited"], 1)

                for tile, name in ((ident, "ident"), (k_decay, "k_decay"), (q_decay, "q_decay"), (decay, "decay"),
                                   (head_rows, "head_rows"), (head_cols, "head_cols"), (chunk_decay, "chunk_decay")):
                    sp.dma_start(tile[:], D[name]).then_inc(S["consts"], 16)
                sp.dma_start(gain_mix[:], D["g_post_mix"].broadcast_to([P, DM])).then_inc(S["consts"], 16)
                sp.dma_start(gain_ffn[:], D["g_pre_ffn"].broadcast_to([P, DM])).then_inc(S["consts"], 16)

                def load_ret(c, s):
                    for n, (at, base, tiles) in enumerate(((0, RQ, 2), (2, RK, 2), (4, RV, 4))):
                        src = D["projT"][base:base + tiles * P, bass.ts(c, P)].rearrange("(k p) t -> p k t", p=P)
                        sp.dma_start(qkv[:, s, at:at + tiles, :], src).then_inc(qkv_loaded[s], 16)

                def load_att(c, s):
                    src = D["att_out"][:, bass.ts(c, P), :].rearrange("a t n -> t a n")
                    sp.dma_start(att_in[:, s], src).then_inc(att_loaded[s], 16)
                    src = D["projT"][RG:RG + WIDTH, bass.ts(c, P)].rearrange("(k p) t -> p k t", p=P)
                    sp.dma_start(gate[:, s], src).then_inc(att_loaded[s], 16)

                load_ret(0, 0)
                load_att(0, 0)
                for k in range(KT):
                    if k:
                        sp.wait_ge(S["w_split"], k)
                    sp.dma_start(w_raw, D["w_out"][k * P:(k + 1) * P, :]).then_inc(S["w_loaded"], 16)

                def step(c, s, on):
                    if on(0) and (not isinstance(c, int) or c + 1 < CHUNKS):
                        if not isinstance(c, int) or c:
                            sp.wait_ge(S["output"], 2 * c)
                            sp.wait_ge(S["lo_b"], c)
                            taken()
                        load_ret(c + 1, 1 - s)
                        load_att(c + 1, 1 - s)
                    if on(LAG_OUT):
                        d = c - LAG_OUT
                        if not isinstance(c, int) or d:
                            sp.wait_ge(S["x1_done"], d)
                            taken()
                        sp.dma_start(xin[:], D["x"][bass.ts(d, P), :]).then_inc(S_x, 16)
                    if on(LAG_H):
                        d = c - LAG_H
                        sp.wait_ge(S["h_lo"], d + 1)
                        taken()
                        for tile, name in ((hT_hi, "h_hi"), (hT_lo, "h_lo")):
                            dst = D[name][:, bass.ts(d, P)].rearrange("(k p) t -> p k t", p=P)
                            sp.dma_start(dst, tile[:].bitcast(F32)).then_inc(h_stored, 16)
                    if on(LAG_OUT):
                        d = c - LAG_OUT
                        sp.wait_ge(S["x1_done"], d + 1)
                        taken()
                        sp.dma_start(D["x1"][bass.ts(d, P), :], x1[:]).then_inc(x1_stored, 16)

                S_x = x_loaded
                steps(sp, step)
                sp.wait_ge(h_stored, 32 * CHUNKS)
                sp.wait_ge(x1_stored, 16 * CHUNKS)

            @block.tensor
            def _(pe):
                pe.wait_ge(S["consts"], 16 * CONSTS)

                def step(c, s, on):
                    if on(0):
                        pe.wait_ge(qkv_loaded[s], 48 * (c // 2) + 48 if isinstance(c, int) else 24 * (c - s) + 48)
                        if not isinstance(c, int) or c:
                            free(pe, c, on, 0)
                        for to, of in enumerate((4, 5, 6, 7, 2, 3)):
                            last = nc.tensor.transpose(tp[:, to, :], qkv[:, s, of, :], ident[:])
                        last.then_inc(S["turned"], 1)
                    if on(LAG_OUT):
                        d = c - LAG_OUT
                        if isinstance(c, int) and d == 0:
                            pe.wait_ge(S["w_split"], KT)
                        pe.wait_ge(S["lo_b"], d + 1)
                        if not isinstance(c, int) or d:
                            pe.wait_ge(S["y_scaled"], d)
                        out_half(0, s)
                    if on(0):
                        for u in range(NU):
                            pe.wait_ge(S["q_ready"], 2 * c + u + 1)
                            if not isinstance(c, int) or c:
                                pe.wait_ge(S["prob_done"], 2 * c + u - 1)
                            nc.tensor.matmul(s_ps[:, u], qkv[:, s, 2 + u, :], q_heads[:, u], start=True, stop=True).then_inc(S["scored"], 1)
                    if on(LAG_MIX):
                        d = c - LAG_MIX
                        pe.wait_ge(S["ret_done"], d + 1)
                        pe.wait_ge(S["att_done"], d + 1)
                        free(pe, c, on, 1)
                        for i in range(4):
                            nc.tensor.transpose(tp[:, i, :], ret[:, i * P:(i + 1) * P], ident[:])
                        for i in range(4):
                            last = nc.tensor.transpose(tp[:, 4 + i, :], parts[:, 0, 2 * i:2 * i + 2, :], ident[:])
                        last.then_inc(S["mix_turned"], 1)
                    if on(LAG_OUT):
                        out_half(1, s).then_inc(S["y_done"], 1)
                    if on(0):
                        first = isinstance(c, int) and c == 0
                        for u in range(NU):
                            pe.wait_ge(S["prob_done"], 2 * c + u + 1)
                            if u == 0:
                                pe.wait_ge(S["v_done"], c + 1)
                                pe.wait_ge(S["q_dec_ready"], c + 1)
                                if first:
                                    pe.wait_ge(S["zeroed"], 3)
                                else:
                                    pe.wait_ge(S["centre_done"], c)
                                    pe.wait_ge(S["state_done"], 2 * c)
                            flat = o_ps[:].rearrange("p h e -> p (h e)")
                            at = u * HU * RET_DV
                            nc.tensor.matmul(flat[:, at:at + HU * RET_DV], q_dec[:, u, :], state[:, s, u, :], start=u == 0, stop=False,
                                             skip_group_check=True)
                            for h in range(HU):
                                to = at + (h // 2) * P
                                of = (u * HU + h) * P - (h % 2) * RET_DV
                                v = v_pad[:, s].rearrange("p h e -> p (h e)")[:, of:of + P]
                                last = nc.tensor.matmul(flat[:, to:to + P], probT[:, u, h, :], v, start=False,
                                                        stop=u == NU - 1 and h == HU - 1, skip_group_check=True)
                            last.then_inc(S["output"], 1)
                        pe.wait_ge(S["k_done"], c + 1)
                        if not first:
                            pe.wait_ge(S["kv_masked"], c)
                        for u in range(NU):
                            v = v_pad[:, s, u * HU:(u + 1) * HU, 0:RET_DV]
                            last = nc.tensor.matmul(kv_ps[:, u, :], k_dec[:, u, :], v, start=u == 0, stop=u == NU - 1, skip_group_check=True)
                        last.then_inc(S["kv_done"], 1)
                    if on(LAG_H):
                        d = c - LAG_H
                        pe.wait_ge(S["h2_done"], d + 1)
                        free(pe, c, on, 2)
                        for i in range(KT):
                            last = nc.tensor.transpose(tp[:, i, :], h2[:, i * P:(i + 1) * P], ident[:])
                        last.then_inc(S["h_turned"], 1)

                def free(pe, c, on, use):
                    if use == 0:
                        if on(LAG_H + 1) and (not isinstance(c, int) or c > LAG_H):
                            pe.wait_ge(S["h_lo"], c - LAG_H)
                        elif on(LAG_MIX + 1) if isinstance(c, int) else True:
                            pe.wait_ge(S["lo_b"], c - 1)
                        else:
                            pe.wait_ge(S["k_done"], c)
                            pe.wait_ge(S["v_done"], c)
                    elif use == 1:
                        if on(0):
                            pe.wait_ge(S["k_done"], c + 1)
                            pe.wait_ge(S["v_done"], c + 1)
                        else:
                            pe.wait_ge(S["h_lo"], c - LAG_H)
                    elif on(LAG_MIX):
                        pe.wait_ge(S["lo_b"], c)
                    else:
                        if isinstance(c, int) and c - LAG_H > 0:
                            pe.wait_ge(S["h_lo"], c - LAG_H)

                def out_half(half, s):
                    n = 0
                    for k in range(KT):
                        for a, w in ((mT_hi, w_hi), (mT_hi, w_lo), (mT_lo, w_hi)):
                            last = nc.tensor.matmul(y_ps[:, half, :], a[:, s, k, :], w[:, k, half * GROUP:(half + 1) * GROUP],
                                                    start=n == 0, stop=n == 3 * KT - 1)
                            n += 1
                    return last

                steps(pe, step)

            @block.vector
            def _(dve):
                for s in range(2):
                    nc.vector.memset(v_pad[:, s], 0.0).then_inc(S["zeroed"], 1)
                nc.vector.memset(state[:, 0], 0.0).then_inc(S["zeroed"], 1)
                dve.wait_ge(S["consts"], 16 * CONSTS)
                for k in range(KT):
                    dve.wait_ge(S["w_loaded"], 16 * k + 16)
                    nc.vector.tensor_copy(w_hi[:, k, :], w_raw).then_inc(S["w_hi_split"], 1)
                    dve.wait_ge(S["w_hi_split"], k + 1)
                    nc.vector.tensor_tensor(w_lo[:, k, :], w_raw, w_hi[:, k, :].bitcast(F32), ALU.subtract).then_inc(S["w_split"], 1)

                def step(c, s, on):
                    static = isinstance(c, int)
                    if on(0):
                        a = att_in[:, s].rearrange("p a (u n) -> p a u n", n=AO_W)
                        maxima, sums = a[:, :, :, 2 * ATT_D:2 * ATT_D + 2], a[:, :, :, 2 * ATT_D + 2:2 * ATT_D + 4]
                        four = lambda t: t.rearrange("p (u h) -> p u h", h=2)
                        dve.wait_ge(att_loaded[s], 32 * (c // 2) + 32 if static else 16 * (c - s) + 32)
                        nc.vector.tensor_tensor(four(att_max[:]), maxima[:, 0], maxima[:, 1], ALU.max).then_inc(S["maxed"], 1)
                        dve.wait_ge(S["maxed"], 2 * c + 1)
                        nc.vector.tensor_tensor(four(att_max[:]), four(att_max[:]), maxima[:, 2], ALU.max).then_inc(S["maxed"], 1)
                        dve.wait_ge(S["maxed"], 2 * c + 2)
                        if not static or c:
                            dve.wait_ge(S["parted"], 3 * c)
                        for p in range(3):
                            last = nc.vector.tensor_tensor(four(weight[:, p, :]), maxima[:, p], four(att_max[:]), ALU.subtract)
                        last.then_inc(S["differed"], 1)
                        dve.wait_ge(S["turned"], c + 1)
                        if not static or c:
                            dve.wait_ge(S["kv_done"], c)
                        nc.vector.tensor_tensor(k_dec[:], tp[:, 4:6, :], k_decay[:], ALU.mult).then_inc(S["k_done"], 1)
                        dve.wait_ge(S["exped"], c + 1)
                        for p in range(3):
                            last = nc.vector.tensor_tensor(four(scaled_sum[:, p, :]), four(weight[:, p, :]), sums[:, p], ALU.mult)
                        last.then_inc(S["dens_done"], 1)
                        dve.wait_ge(S["dens_done"], c + 1)
                        nc.vector.tensor_reduce(sum8[:], scaled_sum[:].rearrange("p a h -> p h a"), AX.X, ALU.add).then_inc(S["sum_done"], 1)
                        dve.wait_ge(S["sum_done"], c + 1)
                        nc.vector.reciprocal(sum8[:], sum8[:]).then_inc(S["recip_done"], 1)
                        dve.wait_ge(S["recip_done"], c + 1)
                        for p in range(3):
                            last = nc.vector.tensor_tensor(weight[:, p, :], weight[:, p, :], sum8[:], ALU.mult)
                        last.then_inc(S["weighted"], 1)
                        for u in range(NU):
                            dve.wait_ge(S["scored"], 2 * c + u + 1)
                            if not static or c:
                                dve.wait_ge(S["output"], 2 * c + u - 1)
                            nc.vector.tensor_tensor(probT[:, u], s_ps[:, u], decay[:, u], ALU.mult).then_inc(S["prob_done"], 1)
                    if on(LAG_MIX):
                        d = c - LAG_MIX
                        dve.wait_ge(S["mix_turned"], d + 1)
                        if not static or d:
                            dve.wait_ge(S["hi_a"], d)
                            dve.wait_ge(S["lo_a"], d)
                        nc.vector.tensor_tensor(mixT[:], tp[:, 0:4, :], gate[:, 1 - s], ALU.mult).then_inc(S["gated"], 1)
                        dve.wait_ge(S["hi_b"], d + 1)
                        nc.vector.tensor_tensor(mT_lo[:, 1 - s, 4:8, :], tp[:, 4:8, :], mT_hi[:, 1 - s, 4:8, :].bitcast(F32),
                                                ALU.subtract).then_inc(S["lo_a"], 1)
                        dve.wait_ge(S["hi_a"], d + 1)
                        nc.vector.tensor_tensor(mT_lo[:, 1 - s, 0:4, :], mixT[:], mT_hi[:, 1 - s, 0:4, :].bitcast(F32),
                                                ALU.subtract).then_inc(S["lo_b"], 1)
                    if on(LAG_OUT):
                        d = c - LAG_OUT
                        dve.wait_ge(S["y_sq"], d + 1)
                        nc.vector.tensor_scalar(ssq[:, 1:2], ssq[:, 0:1], 1.0 / DM, RMS_EPS, ALU.mult, ALU.add).then_inc(S["y_mean"], 1)
                        dve.wait_ge(S["y_root"], d + 1)
                        if not static or d:
                            dve.wait_ge(x1_stored, 16 * d)
                            dve.wait_ge(S["h2_done"], d)
                        nc.vector.scalar_tensor_tensor(x1[:], y_ps[:].rearrange("p a n -> p (a n)"), ssq[:, 1:2], gain_mix[:],
                                                       ALU.mult, ALU.mult).then_inc(S["y_scaled"], 1)
                        dve.wait_ge(S["y_scaled"], d + 1)
                        dve.wait_ge(x_loaded, 16 * d + 16)
                        nc.vector.tensor_tensor(x1[:], x1[:], xin[:], ALU.add).then_inc(S["x1_done"], 1)
                    if on(0):
                        dve.wait_ge(S["output"], 2 * c + 2)
                        nc.vector.tensor_reduce(stat[:, 0, :], o_ps[:], AX.X, ALU.add).then_inc(S["summed"], 1)
                        dve.wait_ge(S["summed"], c + 1)
                        nc.vector.tensor_scalar(stat[:, 1, :], stat[:, 0, :], 1.0 / RET_DV, None, ALU.mult).then_inc(S["meaned"], 1)
                        dve.wait_ge(S["meaned"], c + 1)
                        if not static or c:
                            dve.wait_ge(S["ret_done"], c)
                        nc.vector.tensor_tensor(centred[:], o_ps[:], stat[:, 1, :].unsqueeze(2).broadcast_to([P, RET_HEADS, RET_DV]),
                                                ALU.subtract).then_inc(S["centre_done"], 1)
                        dve.wait_ge(S["kv_done"], c + 1)
                        cols = head_cols[:].unsqueeze(1).broadcast_to([P, NU, HU * RET_DV])
                        nc.vector.tensor_tensor(kv[:], kv_ps[:], cols, ALU.mult).then_inc(S["kv_masked"], 1)
                        dve.wait_ge(S["kv_masked"], c + 1)
                        for u in range(NU):
                            nc.vector.scalar_tensor_tensor(state[:, 1 - s, u, :], state[:, s, u, :], chunk_decay[:, u:u + 1], kv[:, u, :],
                                                           ALU.mult, ALU.add).then_inc(S["state_done"], 1)
                        dve.wait_ge(S["squared"], c + 1)
                        nc.vector.tensor_reduce(stat[:, 2, :], squares[:], AX.X, ALU.add).then_inc(S["var_sum"], 1)
                        dve.wait_ge(S["var_sum"], c + 1)
                        nc.vector.tensor_scalar(stat[:, 2, :], stat[:, 2, :], 1.0 / RET_DV, GN_EPS, ALU.mult, ALU.add).then_inc(S["var_done"], 1)
                    if on(LAG_OUT):
                        d = c - LAG_OUT
                        dve.wait_ge(S["x_sq"], d + 1)
                        nc.vector.tensor_scalar(ssq[:, 3:4], ssq[:, 2:3], 1.0 / DM, RMS_EPS, ALU.mult, ALU.add).then_inc(S["x_mean"], 1)
                        dve.wait_ge(S["x_root"], d + 1)
                        if not static or d:
                            dve.wait_ge(S["h_turned"], d)
                        nc.vector.scalar_tensor_tensor(h2[:], x1[:], ssq[:, 3:4], gain_ffn[:], ALU.mult, ALU.mult).then_inc(S["h2_done"], 1)
                    if on(LAG_H):
                        d = c - LAG_H
                        dve.wait_ge(S["h_hi"], d + 1)
                        nc.vector.tensor_tensor(hT_lo[:], tp[:], hT_hi[:].bitcast(F32), ALU.subtract).then_inc(S["h_lo"], 1)

                steps(dve, step)

            @block.scalar
            def _(act):
                def step(c, s, on):
                    static = isinstance(c, int)
                    if on(0):
                        act.wait_ge(S["differed"], c + 1)
                        nc.scalar.activation(weight[:], weight[:], ACT.Exp, scale=SCALE).then_inc(S["exped"], 1)
                        act.wait_ge(S["turned"], c + 1)
                        if static and c == 0:
                            act.wait_ge(S["zeroed"], 2)
                        v = tp[:, 0:4, :].rearrange("p k (h e) -> p (k h) e", e=RET_DV)
                        nc.scalar.activation(v_pad[:, s, :, 0:RET_DV], v, ACT.Copy).then_inc(S["v_done"], 1)
                    if on(LAG_MIX):
                        d = c - LAG_MIX
                        act.wait_ge(S["mix_turned"], d + 1)
                        if not static or d > 1:
                            act.wait_ge(S["y_done"], d - 1)
                        nc.scalar.activation(mT_hi[:, 1 - s, 4:8, :], tp[:, 4:8, :], ACT.Copy).then_inc(S["hi_b"], 1)
                        act.wait_ge(S["gated"], d + 1)
                        nc.scalar.activation(mT_hi[:, 1 - s, 0:4, :], mixT[:], ACT.Copy).then_inc(S["hi_a"], 1)
                    if on(LAG_OUT):
                        d = c - LAG_OUT
                        act.wait_ge(S["y_done"], d + 1)
                        nc.scalar.activation(row_squares[:, 0, :], y_ps[:].rearrange("p a n -> p (a n)"), ACT.Square,
                                             accum_out=ssq[:, 0:1]).then_inc(S["y_sq"], 1)
                    if on(0):
                        act.wait_ge(S["centre_done"], c + 1)
                        nc.scalar.activation(squares[:], centred[:], ACT.Square).then_inc(S["squared"], 1)
                    if on(LAG_OUT):
                        act.wait_ge(S["x1_done"], d + 1)
                        nc.scalar.activation(row_squares[:, 1, :], x1[:], ACT.Square, accum_out=ssq[:, 2:3]).then_inc(S["x_sq"], 1)
                    if on(LAG_H):
                        d = c - LAG_H
                        act.wait_ge(S["h_turned"], d + 1)
                        if not static or d:
                            act.wait_ge(h_stored, 32 * d)
                        nc.scalar.activation(hT_hi[:], tp[:], ACT.Copy).then_inc(S["h_hi"], 1)

                steps(act, step)

            @block.gpsimd
            def _(pool):
                nc.gpsimd.memset(minus_half[:], -0.5).then_inc(S["half_set"], 1)
                pool.wait_ge(S["half_set"], 1)
                pool.wait_ge(S["consts"], 16 * CONSTS)

                def step(c, s, on):
                    static = isinstance(c, int)
                    if on(0):
                        pool.wait_ge(qkv_loaded[s], 48 * (c // 2) + 48 if static else 24 * (c - s) + 48)
                        if not static or c:
                            pool.wait_ge(S["output"], 2 * c)
                        for u in range(NU):
                            q = qkv[:, s, u, :].unsqueeze(1).broadcast_to([P, HU, P])
                            rows = head_rows[:].unsqueeze(2).broadcast_to([P, HU, P])
                            nc.gpsimd.tensor_tensor(q_heads[:, u], q, rows, ALU.mult).then_inc(S["q_ready"], 1)
                        nc.gpsimd.tensor_tensor(q_dec[:], qkv[:, s, 0:NU, :], q_decay[:], ALU.mult).then_inc(S["q_dec_ready"], 1)
                    if on(LAG_OUT):
                        d = c - LAG_OUT
                        pool.wait_ge(S["y_mean"], d + 1)
                        nc.gpsimd.tensor_tensor(ssq[:, 1:2], ssq[:, 1:2], minus_half[:, 0:1], ALU.pow).then_inc(S["y_root"], 1)
                    if on(0):
                        pool.wait_ge(S["weighted"], c + 1)
                        if static and c == 0:
                            pool.wait_ge(S["w_split"], KT)
                        else:
                            pool.wait_ge(S["mix_turned"], c)
                        for p in range(3):
                            four = lambda t: t.rearrange("p (u h) d -> p u h d", h=2)
                            part = att_in[:, s, p, :].rearrange("p (u n) -> p u n", n=AO_W)[:, :, 0:2 * ATT_D]
                            w = weight[:, p, :].rearrange("p (u h) -> p u h", h=2).unsqueeze(3).broadcast_to([P, 4, 2, ATT_D])
                            nc.gpsimd.tensor_tensor(four(parts[:, p]), part.rearrange("p u (h d) -> p u h d", h=2), w,
                                                    ALU.mult).then_inc(S["parted"], 1)
                        pool.wait_ge(S["parted"], 3 * c + 2)
                        nc.gpsimd.tensor_tensor(parts[:, 0], parts[:, 0], parts[:, 1], ALU.add).then_inc(S["parts_a"], 1)
                        pool.wait_ge(S["parts_a"], c + 1)
                        pool.wait_ge(S["parted"], 3 * c + 3)
                        nc.gpsimd.tensor_tensor(parts[:, 0], parts[:, 0], parts[:, 2], ALU.add).then_inc(S["att_done"], 1)
                        pool.wait_ge(S["var_done"], c + 1)
                        nc.gpsimd.tensor_tensor(stat[:, 3, :], stat[:, 2, :], minus_half[:], ALU.pow).then_inc(S["rooted"], 1)
                        pool.wait_ge(S["rooted"], c + 1)
                        r = stat[:, 3, :].unsqueeze(2).broadcast_to([P, RET_HEADS, RET_DV])
                        nc.gpsimd.tensor_tensor(ret[:].rearrange("p (h e) -> p h e", e=RET_DV), centred[:], r,
                                                ALU.mult).then_inc(S["ret_done"], 1)
                    if on(LAG_OUT):
                        pool.wait_ge(S["x_mean"], d + 1)
                        nc.gpsimd.tensor_tensor(ssq[:, 3:4], ssq[:, 3:4], minus_half[:, 0:1], ALU.pow).then_inc(S["x_root"], 1)

                steps(pool, step)


def ffn(nc, D):
    TILES = 2
    PW = TILES * P
    PARTS = D_FF // PW
    HALVES = 2
    HALF = SEQ // HALVES
    UG = HALF // GROUP
    UC = GROUP // P
    with ExitStack() as ctx:
        m = Mem(nc, ctx, "ff")
        h_hi = m.sb("h_hi", [P, KT, HALF], F32R)
        h_lo = m.sb("h_lo", [P, KT, HALF], F32R)
        total = m.sb("total", [P, UG * UC, DM])
        raw = m.sb("raw", [P, 2, KT, PW])
        w_hi = m.sb("w_hi", [P, 2, KT, PW], F32R)
        w_lo = m.sb("w_lo", [P, 2, KT, PW], F32R)
        down_raw = m.sb("down_raw", [P, TILES, DM])
        down_hi = m.sb("down_hi", [P, TILES, DM], F32R)
        down_lo = m.sb("down_lo", [P, TILES, DM], F32R)
        gated = m.sb("gated", [P, TILES, GROUP])
        a_hi = m.sb("a_hi", [P, UG, TILES, GROUP], F32R)
        a_lo = m.sb("a_lo", [P, UG, TILES, GROUP], F32R)
        gain = m.sb("gain", [P, DM])
        x1 = m.sb("x1", [P, 2, DM])
        squares = m.sb("squares", [P, DM])
        ssq = m.sb("ssq", [P, UC])
        minus_half = m.sb("minus_half", [P, UC])
        gu_ps = m.ps("gu", [P, TILES, 2, GROUP])
        d_ps = m.ps("down", [P, 2, DM])
        gain_loaded, half_set = m.sem("gain_loaded"), m.sem("half_set")
        h_loaded = m.sems("h_loaded", UG)
        gu_loaded, down_loaded = m.sem("gu_loaded"), m.sem("down_loaded")
        gu_hi, gu_split, down_his, down_split = m.sem("gu_hi"), m.sem("gu_split"), m.sem("down_his"), m.sem("down_split")
        gu_done, silu_done, mul_done = m.sem("gu_done"), m.sem("silu_done"), m.sem("mul_done")
        a_hi_done, a_lo_done = m.sem("a_hi_done"), m.sem("a_lo_done")
        down_done, added = m.sem("down_done"), m.sem("added")
        squared, meaned, rooted = m.sem("squared"), m.sem("meaned"), m.sem("rooted")
        scaled, out_done = m.sem("scaled"), m.sem("out_done")
        x1_loaded, out_stored = m.sems("x1_loaded", 2), m.sems("out_stored", 2)
        B = 2
        UNITS = HALVES * PARTS * UG

        def parts(eng, part):
            for half in range(HALVES):
                at = half * PARTS
                part(at, True, False, half)
                part(at + 1, False, False, half)
                with eng.Fori(at + 2, at + PARTS - 1) as J:
                    part(J, False, False, half)
                part(at + PARTS - 1, False, True, half)

        with nc.Block() as block:

            @block.sync
            def _(sp):
                def load_gu(j):
                    for n, w in enumerate(("w_gate", "w_up")):
                        src = D[w][:, bass.ts(j, PW)].rearrange("(k p) n -> p k n", p=P)
                        sp.dma_start(raw[:, n], src).then_inc(gu_loaded, 16)

                def load_down(j):
                    sp.dma_start(down_raw[:], D["w_down"][bass.ts(j, PW), :].rearrange("(t p) n -> p t n", p=P)).then_inc(down_loaded, 16)

                def load_h(half, g):
                    t = slice(half * HALF + g * GROUP, half * HALF + (g + 1) * GROUP)
                    for tile, name in ((h_hi, "h_hi"), (h_lo, "h_lo")):
                        for k in range(0, KT, KT // 2):
                            src = D[name][k * P:(k + KT // 2) * P, t].rearrange("(k p) t -> p k t", p=P)
                            sp.dma_start(tile[:, k:k + KT // 2, g * GROUP:(g + 1) * GROUP].bitcast(F32), src).then_inc(h_loaded[g], 16)

                def load_x1(n):
                    if n >= 2:
                        sp.wait_ge(out_stored[n % 2], 16 * (n // 2))
                    sp.dma_start(x1[:, n % 2], D["x1"][bass.ts(n, P), :]).then_inc(x1_loaded[n % 2], 16)

                def finish(half, g):
                    for c in range(UC):
                        n = (half * UG + g) * UC + c
                        sp.wait_ge(out_done, n + 1)
                        sp.dma_start(D["out"][n * P:(n + 1) * P, :], x1[:, n % 2]).then_inc(out_stored[n % 2], 16)
                        if n + 2 < HALVES * UG * UC:
                            load_x1(n + 2)

                load_gu(0)
                load_h(0, 0)
                sp.dma_start(gain[:], D["g_post_ffn"].broadcast_to([P, DM])).then_inc(gain_loaded, 16)
                load_down(0)
                load_h(0, 1)
                load_x1(0)
                load_x1(1)

                def part(J, first, last, half):
                    if not (last and half == HALVES - 1):
                        sp.wait_ge(gu_split, 4 * J + 4)
                        load_gu(0 if last else J + 1 - half * PARTS)
                    if first and half:
                        finish(half - 1, 1)
                    if last and half < HALVES - 1:
                        sp.wait_ge(gu_done, 8 * J + 4)
                        load_h(half + 1, 0)
                    if not (last and half == HALVES - 1):
                        sp.wait_ge(down_split, 2 * J + 2)
                        load_down(0 if last else J + 1 - half * PARTS)
                    if last:
                        if half < HALVES - 1:
                            sp.wait_ge(gu_done, 8 * J + 8)
                            load_h(half + 1, 1)
                        finish(half, 0)

                parts(sp, part)
                finish(HALVES - 1, 1)
                for s in range(2):
                    sp.wait_ge(out_stored[s], 16 * HALVES * UG * UC // 2)

            @block.tensor
            def _(pe):
                pe.sem_inc(added, B)

                def gate_up(J, g, first, half):
                    u = 2 * J + g
                    if first:
                        pe.wait_ge(h_loaded[g], 64 * (half + 1))
                    t = slice(g * GROUP, (g + 1) * GROUP)
                    for tile in range(TILES):
                        cols = slice(tile * P, (tile + 1) * P)
                        for n, free in ((0, silu_done), (1, mul_done)):
                            if g == 0:
                                pe.wait_ge(gu_split, 4 * J + 2 * tile + n + 1)
                            if not (first and half == 0 and g == 0):
                                pe.wait_ge(free, 2 * u - 1 + tile)
                            i = 0
                            for k in range(KT):
                                for w, h in ((w_hi, h_hi), (w_hi, h_lo), (w_lo, h_hi)):
                                    last = nc.tensor.matmul(gu_ps[:, tile, n], w[:, n, k, cols], h[:, k, t],
                                                            start=i == 0, stop=i == 3 * KT - 1)
                                    i += 1
                            last.then_inc(gu_done, 1)

                def down(J, g):
                    u = 2 * J + g
                    pe.wait_ge(a_hi_done, 2 * u + 2)
                    pe.wait_ge(a_lo_done, 2 * u + 2)
                    if g == 0:
                        pe.wait_ge(down_split, 2 * J + 2)
                    for c in range(UC):
                        pe.wait_ge(added, 4 * u + c - B + 1 + B)
                        for half in range(2):
                            i = 0
                            for tile in range(TILES):
                                for a, w in ((a_hi, down_hi), (a_hi, down_lo), (a_lo, down_hi)):
                                    last = nc.tensor.matmul(d_ps[:, c % 2, half * GROUP:(half + 1) * GROUP],
                                                            a[:, g, tile, c * P:(c + 1) * P],
                                                            w[:, tile, half * GROUP:(half + 1) * GROUP],
                                                            start=i == 0, stop=i == 3 * TILES - 1)
                                    i += 1
                        last.then_inc(down_done, 1)

                def part(J, first, last, half):
                    gate_up(J, 0, first, half)
                    if not (first and half == 0):
                        down(J - 1, 1)
                    gate_up(J, 1, first, half)
                    down(J, 0)

                parts(pe, part)
                down(HALVES * PARTS - 1, 1)

            @block.scalar
            def _(act):
                def split_gu(J, i):
                    tile, n = i // 2, i % 2
                    cols = slice(tile * P, (tile + 1) * P)
                    act.wait_ge(gu_loaded, 32 * J + 32)
                    if not (isinstance(J, int) and J == 0):
                        act.wait_ge(gu_done, 8 * J - 4 + i + 1)
                    nc.scalar.activation(w_hi[:, n, :, cols], raw[:, n, :, cols], ACT.Copy).then_inc(gu_hi, 1)

                def split_down(J):
                    act.wait_ge(down_loaded, 16 * J + 16)
                    if not (isinstance(J, int) and J == 0):
                        act.wait_ge(down_done, 8 * J)
                    for tile in range(TILES):
                        nc.scalar.activation(down_hi[:, tile], down_raw[:, tile], ACT.Copy).then_inc(down_his, 1)

                def products(J, g, tile):
                    u = 2 * J + g
                    act.wait_ge(gu_done, 4 * u + 2 * tile + 1)
                    if not (isinstance(u, int) and u == 0):
                        act.wait_ge(a_lo_done, 2 * u - 1 + tile)
                    nc.scalar.activation(gated[:, tile], gu_ps[:, tile, 0], ACT.Silu).then_inc(silu_done, 1)
                    act.wait_ge(mul_done, 2 * u + tile + 1)
                    nc.scalar.activation(a_hi[:, g, tile], gated[:, tile], ACT.Copy).then_inc(a_hi_done, 1)

                def finish(half, g):
                    for c in range(UC):
                        n = (half * UG + g) * UC + c
                        u = (half * PARTS + PARTS - 1) * UG + g
                        act.wait_ge(added, 4 * u + c + 1 + B)
                        if n:
                            act.wait_ge(squared, n)
                        if n >= UC and c == 0:
                            act.wait_ge(scaled, n)
                        nc.scalar.activation(squares[:], total[:, g * UC + c], ACT.Square,
                                             accum_out=ssq[:, c:c + 1]).then_inc(squared, 1)

                for i in range(2 * TILES):
                    split_gu(0, i)

                def part(J, first, last, half):
                    for g in range(UG):
                        if g == 1:
                            split_down(J)
                        products(J, g, 0)
                        more = g == 1 and not (last and half == HALVES - 1)
                        if more:
                            split_gu(J + 1, 0)
                            split_gu(J + 1, 1)
                        products(J, g, 1)
                        if more:
                            split_gu(J + 1, 2)
                            split_gu(J + 1, 3)
                        if first and half and g == 0:
                            finish(half - 1, 1)
                        if last and g == 1:
                            finish(half, 0)

                parts(act, part)
                finish(HALVES - 1, 1)

            @block.gpsimd
            def _(pool):
                nc.gpsimd.memset(minus_half[:], -0.5).then_inc(half_set, 1)
                pool.wait_ge(half_set, 1)
                for n in range(HALVES * UG):
                    pool.wait_ge(meaned, n + 1)
                    nc.gpsimd.tensor_tensor(ssq[:], ssq[:], minus_half[:], ALU.pow).then_inc(rooted, 1)

            @block.vector
            def _(dve):
                dve.wait_ge(gain_loaded, 16)

                def split_gu(J, i):
                    tile, n = i // 2, i % 2
                    cols = slice(tile * P, (tile + 1) * P)
                    dve.wait_ge(gu_hi, 4 * J + i + 1)
                    nc.vector.tensor_tensor(w_lo[:, n, :, cols], raw[:, n, :, cols], w_hi[:, n, :, cols].bitcast(F32),
                                            ALU.subtract).then_inc(gu_split, 1)

                def split_down(J):
                    for tile in range(TILES):
                        dve.wait_ge(down_his, 2 * J + tile + 1)
                        nc.vector.tensor_tensor(down_lo[:, tile], down_raw[:, tile], down_hi[:, tile].bitcast(F32),
                                                ALU.subtract).then_inc(down_split, 1)

                def products(J, g, tile):
                    u = 2 * J + g
                    dve.wait_ge(silu_done, 2 * u + tile + 1)
                    dve.wait_ge(gu_done, 4 * u + 2 * tile + 2)
                    nc.vector.tensor_tensor(gated[:, tile], gated[:, tile], gu_ps[:, tile, 1], ALU.mult).then_inc(mul_done, 1)
                    dve.wait_ge(a_hi_done, 2 * u + tile + 1)
                    nc.vector.tensor_tensor(a_lo[:, g, tile], gated[:, tile], a_hi[:, g, tile].bitcast(F32),
                                            ALU.subtract).then_inc(a_lo_done, 1)

                def add(J, g, fresh):
                    for c in range(UC):
                        d = 4 * (2 * J + g) + c
                        dve.wait_ge(down_done, d + 1)
                        to = total[:, g * UC + c]
                        if fresh:
                            nc.vector.tensor_copy(to, d_ps[:, c % 2]).then_inc(added, 1)
                        else:
                            dve.wait_ge(added, d - 8 + 1 + B)
                            nc.vector.tensor_tensor(to, to, d_ps[:, c % 2], ALU.add).then_inc(added, 1)

                def finish(half, g):
                    n0 = (half * UG + g) * UC
                    dve.wait_ge(squared, n0 + UC)
                    nc.vector.tensor_scalar(ssq[:], ssq[:], 1.0 / DM, RMS_EPS, ALU.mult, ALU.add).then_inc(meaned, 1)
                    dve.wait_ge(rooted, half * UG + g + 1)
                    for c in range(UC):
                        t = total[:, g * UC + c]
                        nc.vector.scalar_tensor_tensor(t, t, ssq[:, c:c + 1], gain[:], ALU.mult, ALU.mult).then_inc(scaled, 1)
                    for c in range(UC):
                        n = n0 + c
                        dve.wait_ge(scaled, n + 1)
                        dve.wait_ge(x1_loaded[n % 2], 16 * (n // 2) + 16)
                        nc.vector.tensor_tensor(x1[:, n % 2], x1[:, n % 2], total[:, g * UC + c], ALU.add).then_inc(out_done, 1)

                for i in range(2 * TILES):
                    split_gu(0, i)

                def part(J, first, last, half):
                    for g in range(UG):
                        if g == 1:
                            split_down(J)
                        products(J, g, 0)
                        more = g == 1 and not (last and half == HALVES - 1)
                        if more:
                            split_gu(J + 1, 0)
                            split_gu(J + 1, 1)
                        products(J, g, 1)
                        if g == 0:
                            if not (first and half == 0):
                                add(J - 1, 1, J == half * PARTS + 1 if isinstance(J, int) else False)
                        else:
                            add(J, 0, first)
                        if more:
                            split_gu(J + 1, 2)
                            split_gu(J + 1, 3)
                        if first and half and g == 0:
                            finish(half - 1, 1)
                        if last and g == 1:
                            finish(half, 0)

                parts(dve, part)
                add(HALVES * PARTS - 1, 1, False)
                finish(HALVES - 1, 1)


INPUTS = ["x", "positions", "w_in", "w_out", "g_pre_mix", "g_post_mix", "g_pre_ffn", "g_post_ffn",
          "w_gate", "w_up", "w_down"]


def tensors(nc, aps, given=()):
    D = {"x": aps["in_x"][0], "positions": aps["in_positions"]}
    if "out" in aps:
        D["out"] = aps["out"][0]
    for n in ("w_in", "w_out", "w_gate", "w_up", "w_down"):
        D[n] = aps[f"in_{n}"][0]
    for n in ("g_pre_mix", "g_post_mix", "g_pre_ffn", "g_post_ffn"):
        D[n] = aps[f"in_{n}"]
    for n in aps:
        if n.startswith("const_"):
            D[n[6:]] = aps[n]
    for n, shape in (("projT", (PROJ, SEQ)), ("att_out", (3, SEQ, ATT_HEADS // 2 * AO_W)), ("x1", (SEQ, DM)), ("h_hi", (DM, SEQ)), ("h_lo", (DM, SEQ))):
        if n in aps:
            D[n] = aps[n]
        else:
            D[n] = nc.dram_tensor(n, shape, F32, kind="Internal").ap()
    for n in ("rot_hi", "rot_lo"):
        D[n] = aps[n] if n in aps else nc.dram_tensor(n, (2 * WIDTH, SEQ), F32, kind="Internal").ap()
    return D


def build(nc, aps):
    D = tensors(nc, aps)
    with ExitStack() as ctx:
        keep = {n: ctx.enter_context(nc.sbuf_tensor(n, [P, KT, SEQ], F32R)) for n in ("hT_hi", "hT_lo")}
        normed_transpose(nc, D, keep)
        project(nc, D, keep)
    attention(nc, D)
    mix(nc, D)
    ffn(nc, D)




def constants():
    import numpy as np

    c = {"ident": np.eye(P, dtype=np.float32)}
    a, k = np.arange(P)[:, None], np.arange(P)[None, :]
    c["mask"] = np.where(np.concatenate([k >= a, k <= a], 1), 0.0, NEG).astype(np.float32)
    f = np.float32(500000.0) ** (-np.arange(0, ROPE, 2, dtype=np.float32) / np.float32(ROPE))
    att = np.zeros((ATT_D, 2), np.float32)
    att[:ROPE, 0] = np.tile(f, 2)
    att[:ROPE, 1] = np.repeat([-1.0, 1.0], ROPE // 2)
    f = np.float32(1.0) / np.float32(10000.0) ** np.linspace(0, 1, RET_DK // 2, dtype=np.float32)
    ret = np.stack([np.tile(f, 2), np.repeat([-1.0, 1.0], RET_DK // 2)], 1).astype(np.float32)
    c["rotation"] = np.concatenate([np.tile(att, (P // ATT_D, 1)), np.tile(ret, (P // RET_DK, 1))], 1)
    log_g = np.log1p(-np.exp2(-5.0 - np.arange(RET_HEADS, dtype=np.float32))).astype(np.float32).reshape(2, 4)
    i = np.arange(P, dtype=np.float32)
    scale = RET_DK ** -0.5
    c["k_decay"] = np.repeat(np.exp(log_g[None] * (P - 1.0 - i)[:, None, None]) * scale, RET_DK, 2)
    c["q_decay"] = np.repeat(np.exp(log_g[:, :, None] * (i + 1.0)), RET_DK, 1).transpose(1, 0, 2)
    ahead = i[None, :] - i[:, None]
    c["decay"] = np.where(ahead >= 0, np.exp(log_g[:, :, None, None] * np.maximum(ahead, 0.0)), 0.0).transpose(2, 0, 1, 3) * scale
    row = np.arange(P)[:, None] // RET_DK
    c["head_rows"] = (row == np.arange(4)[None]).astype(np.float32)
    c["head_cols"] = (row == np.arange(4 * RET_DV)[None] // RET_DV).astype(np.float32)
    c["chunk_decay"] = np.repeat(np.exp(log_g * P), RET_DK, 1).T
    return {n: np.ascontiguousarray(a, dtype=np.float32) for n, a in c.items()}


def kernel(**inputs):
    import numpy as np
    import concourse.bacc as bacc
    from concourse.bass_utils import run_bass_kernel_spmd

    arrays = {f"in_{n}": np.ascontiguousarray(inputs[n]) for n in INPUTS}
    arrays.update({f"const_{n}": a for n, a in constants().items()})
    nc = bacc.Bacc("TRN2", target_bir_lowering=False, num_devices=1)
    aps = {n: nc.dram_tensor(n, a.shape, mybir.dt.from_np(a.dtype), kind="ExternalInput").ap() for n, a in arrays.items()}
    aps["out"] = nc.dram_tensor("out", (1, SEQ, DM), F32, kind="ExternalOutput").ap()
    build(nc, aps)
    r = run_bass_kernel_spmd(nc, [arrays], core_ids=[0])
    return r.results[0]["out"]
```

```python
import math
from contextlib import ExitStack

import concourse.bass as bass
from concourse import mybir

F32 = mybir.dt.float32
F32R = mybir.dt.float32r
I32 = mybir.dt.int32
ACT = mybir.ActivationFunctionType
ALU = mybir.AluOpType
AX = mybir.AxisListType

P = 128
SEQ = 2048
DM = 1024
KT = DM // P
CHUNKS = SEQ // P
GROUP = 512
GROUPS = SEQ // GROUP
RET_HEADS, RET_DK, RET_DV = 8, 32, 64
ATT_HEADS, ATT_D = 8, 64
RET_QK = RET_HEADS * RET_DK
WIDTH = RET_HEADS * RET_DV
PROJ = 2 * RET_QK + 5 * WIDTH
RQ, RK, RV, RG = 0, RET_QK, 2 * RET_QK, 2 * RET_QK + WIDTH
AQ = RG + WIDTH
AK, AV = AQ + WIDTH, AQ + 2 * WIDTH
ROPE = ATT_D // 4
D_FF = 2816
PATTERNS = (1, 4, 16)
RMS_EPS, GN_EPS = 1e-6, 1e-5
NEG = -1e30
AO_W = 2 * ATT_D + 4


class Mem:

    def __init__(self, nc, ctx, phase):
        self.nc, self.ctx, self.phase = nc, ctx, phase

    def sb(self, name, shape, dt=F32):
        return self.ctx.enter_context(self.nc.sbuf_tensor(f"{self.phase}_{name}", shape, dt))

    def ps(self, name, shape, dt=F32):
        return self.ctx.enter_context(self.nc.psum_tensor(f"{self.phase}_psum_{name}", shape, dt))

    def sem(self, name):
        return self.nc.alloc_semaphore(f"{self.phase}_{name}")

    def sems(self, name, n):
        return [self.sem(f"{name}{i}") for i in range(n)]


def normed_transpose(nc, D, keep):
    hT_hi, hT_lo = keep["hT_hi"], keep["hT_lo"]
    NX = 4
    with ExitStack() as ctx:
        m = Mem(nc, ctx, "nt")
        ident = m.sb("ident", [P, P])
        gain = m.sb("gain", [P, DM])
        minus_half = m.sb("minus_half", [P, 1])
        xin = m.sb("xin", [P, NX, DM])
        xn = m.sb("xn", [P, 2, DM])
        squares = m.sb("squares", [P, 2, DM])
        sumsq = m.sb("sumsq", [P, NX])
        meansq = m.sb("meansq", [P, NX])
        rstd = m.sb("rstd", [P, NX])
        tp = m.ps("tp", [P, 2, KT, P])
        consts, w_loaded = m.sem("consts"), m.sem("w_loaded")
        half_set = m.sem("half_set")
        loaded = m.sems("loaded", NX)
        summed, meaned, rooted, normed = m.sem("summed"), m.sem("meaned"), m.sem("rooted"), m.sem("normed")
        transposed, hi_done, lo_done = m.sem("transposed"), m.sem("hi_done"), m.sem("lo_done")

        def steps(eng, step, lag=0):
            for c in range(NX):
                step(c, c, c % 2, True)
            with eng.Fori(0, CHUNKS // NX - 1) as it:
                for i in range(NX):
                    step(NX * it + (NX + i), i, i % 2, False)
            for c in range(CHUNKS, CHUNKS + lag):
                step(c, c % NX, c % 2, False)

        def has(c, lag):
            return not isinstance(c, int) or 0 <= c - lag < CHUNKS

        def later(c, n):
            return not isinstance(c, int) or c >= n

        with nc.Block() as block:

            @block.sync
            def _(sp):
                def step(c, x, s, early):
                    if not early:
                        sp.wait_ge(normed, c - NX + 1)
                    sp.dma_start(xin[:, x, :], D["x"][bass.ts(c, P), :]).then_inc(loaded[x], 16)
                    if isinstance(c, int) and c == 0:
                        sp.dma_start(gain[:], D["g_pre_mix"].broadcast_to([P, DM])).then_inc(consts, 16)
                        sp.dma_start(ident[:], D["ident"]).then_inc(consts, 16)

                steps(sp, step)
                first = SECTIONS[0][0] * 2 * P
                sp.dma_start(keep["w_raw"][:], D["w_in"][:, first:first + P].rearrange("(k p) n -> p k n", p=P)).then_inc(w_loaded, 16)
                sp.wait_ge(w_loaded, 16)

            @block.scalar
            def _(act):
                def step(c, x, s, early):
                    if has(c, 0):
                        if early:
                            act.wait_ge(loaded[x], 16)
                        else:
                            act.wait_ge(loaded[x], 4 * (c - x) + 16)
                            act.wait_ge(meaned, c - NX + 1)
                        if later(c, 2):
                            act.wait_ge(summed, c - 1)
                        nc.scalar.activation(squares[:, s, :], xin[:, x, :], ACT.Square,
                                             accum_out=sumsq[:, x:x + 1]).then_inc(summed, 1)
                    if has(c, 2):
                        act.wait_ge(transposed, c - 1)
                        nc.scalar.activation(hT_hi[:, :, bass.ts(c - 2, P)], tp[:, s], ACT.Copy).then_inc(hi_done, 1)

                steps(act, step, 2)

            @block.gpsimd
            def _(pool):
                nc.gpsimd.memset(minus_half[:], -0.5).then_inc(half_set, 1)
                pool.wait_ge(half_set, 1)

                def step(c, x, s, early):
                    pool.wait_ge(meaned, c + 1)
                    nc.gpsimd.tensor_tensor(rstd[:, x:x + 1], meansq[:, x:x + 1], minus_half[:], ALU.pow).then_inc(rooted, 1)

                steps(pool, step)

            @block.vector
            def _(dve):
                dve.wait_ge(consts, 32)

                def step(c, x, s, early):
                    if has(c, 1):
                        dve.wait_ge(rooted, c)
                        if later(c - 1, 2):
                            dve.wait_ge(transposed, c - 2)
                        before = (x - 1) % NX
                        nc.vector.scalar_tensor_tensor(xn[:, 1 - s, :], xin[:, before, :], rstd[:, before:before + 1], gain[:],
                                                       ALU.mult, ALU.mult).then_inc(normed, 1)
                    if has(c, 0):
                        dve.wait_ge(summed, c + 1)
                        nc.vector.tensor_scalar(meansq[:, x:x + 1], sumsq[:, x:x + 1], 1.0 / DM, RMS_EPS,
                                                ALU.mult, ALU.add).then_inc(meaned, 1)
                    if has(c, 2):
                        dve.wait_ge(hi_done, c - 1)
                        nc.vector.tensor_tensor(hT_lo[:, :, bass.ts(c - 2, P)], tp[:, s],
                                                hT_hi[:, :, bass.ts(c - 2, P)].bitcast(F32),
                                                ALU.subtract).then_inc(lo_done, 1)

                steps(dve, step, 2)

            @block.tensor
            def _(pe):
                pe.wait_ge(consts, 32)

                def step(c, x, s, early):
                    if has(c, 1):
                        pe.wait_ge(normed, c)
                        if later(c - 1, 2):
                            pe.wait_ge(lo_done, c - 2)
                        for k in range(KT):
                            last = nc.tensor.transpose(tp[:, 1 - s, k, :], xn[:, 1 - s, k * P:(k + 1) * P], ident[:])
                        last.then_inc(transposed, 1)

                steps(pe, step, 1)


def turns_parts():
    left, parts = 2 * math.pi, []
    for _ in range(3):
        unit = 2.0 ** (math.floor(math.log2(left)) - 7)
        parts.append(math.floor(left / unit) * unit)
        left -= parts[-1]
    return parts + [left]


SECTIONS = ((RV // 256, 2, "copy"), (RG // 256, 2, "silu"), (RQ // 256, 2, "ret"), (AQ // 256, 4, "att"),
            (AV // 256, 2, "copy"))


def project(nc, D, keep):
    hT_hi, hT_lo = keep["hT_hi"], keep["hT_lo"]
    pairs = PROJ // (2 * P)
    NR = 4
    C_ADDED = 2
    SWAP = {"ret": [(i + RET_DK // 2) % RET_DK for i in range(RET_DK)],
            "att": [(i + ROPE // 2) % ROPE if i < ROPE else i for i in range(32)]}
    with ExitStack() as ctx:
        m = Mem(nc, ctx, "pr")
        raw = keep["w_raw"]
        w_hi = m.sb("w_hi", [P, 2, KT, P], F32R)
        w_lo = m.sb("w_lo", [P, 2, KT, P], F32R)
        rows = m.sb("rows", [P, NR, GROUP])
        swap = m.sb("swap", [P, 2, GROUP])
        hi = m.sb("hi", [P, 2, GROUP], F32R)
        lo = m.sb("lo", [P, 2, GROUP], F32R)
        rotation = m.sb("rotation", [P, 4])
        quarter = m.sb("quarter", [P, 1])
        part = m.sb("part", [P, SEQ // 2])
        table = {kind: (m.sb(f"cos_{kind}", [P, SEQ]), m.sb(f"sin_{kind}", [P, SEQ])) for kind in ("ret", "att")}
        acc = m.ps("acc", [P, 2, GROUPS, GROUP])
        w_loaded, split = m.sem("w_loaded"), m.sem("split")
        hi_split = m.sem("hi_split")
        tile_done = m.sem("tile_done")
        group_done = m.sem("group_done")
        copied = m.sem("copied")
        row_free = m.sems("row_free", NR)
        shuffled, scaled, added, hi_done, lo_done = m.sem("shuffled"), m.sem("scaled"), m.sem("added"), m.sem("hi_done"), m.sem("lo_done")
        scaled0 = m.sem("scaled0")
        waited = m.sem("waited")
        parts_stored = m.sems("parts_stored", 2)
        consts, angle_step, tables_done = m.sem("consts"), m.sem("angle_step"), m.sem("tables_done")
        angles = m.sems("angles", 2)

        def sections():
            pos = 0
            for first, n, kind in SECTIONS:
                yield kind, first, first + n, pos - first
                pos += n

        ROT0 = 4
        ATT0 = 6

        with nc.Block() as block:

            @block.sync
            def _(sp):
                sp.sem_inc(w_loaded, 16)
                sp.dma_start(rotation[:], D["rotation"]).then_inc(consts, 16)
                for kind in ("ret", "att"):
                    sp.dma_start(table[kind][1][:].bitcast(I32), D["positions"].broadcast_to([P, SEQ])).then_inc(consts, 16)

                def load(column):
                    sp.dma_start(raw[:], D["w_in"][:, bass.ds(column, P)].rearrange("(k p) n -> p k n", p=P)).then_inc(w_loaded, 16)

                tiles = [2 * pair + s for first, n, _ in SECTIONS for pair in range(first, first + n) for s in range(2)]
                sp.wait_ge(split, 1)
                load(tiles[1] * P)
                flat = list(sections())
                for n, (kind, first, end, shift) in enumerate(flat):
                    def body(pair, following):
                        pos = pair + shift
                        for s in range(2):
                            for g in range(GROUPS):
                                t = slice(g * GROUP, (g + 1) * GROUP)
                                at = bass.ds(pair * 2 * P + s * P, P)
                                i = s * GROUPS + g
                                if kind == "att":
                                    a = 8 * (pos - ATT0) + i
                                    sp.wait_ge(lo_done, a + 1)
                                    to = bass.ds(pair * 2 * P + s * P - AQ, P)
                                    sp.dma_start(D["rot_hi"][to, t], hi[:, i % 2, :].bitcast(F32)).then_inc(parts_stored[i % 2], 16)
                                    sp.dma_start(D["rot_lo"][to, t], lo[:, i % 2, :].bitcast(F32)).then_inc(parts_stored[i % 2], 16)
                                else:
                                    if kind == "ret":
                                        sp.wait_ge(added, 8 * (pos - ROT0) + i + 1 + C_ADDED)
                                    else:
                                        sp.wait_ge(copied, 8 * pos + i + 1 + 8)
                                    sp.dma_start(D["projT"][at, t], rows[:, i % NR, :]).then_inc(row_free[i % NR], 16)
                            if following is not None:
                                sp.wait_ge(split, 2 * pos + s + 2)
                                load(following * 2 * P + s * P)

                    if end - first > 1:
                        with sp.Fori(first, end - 1) as pair:
                            body(pair, pair + 1)
                    body(end - 1, flat[n + 1][1] if n + 1 < len(flat) else None)
                for r in range(NR):
                    sp.wait_ge(row_free[r], 16 * (8 * pairs // NR) + 16)
                for r in range(2):
                    sp.wait_ge(parts_stored[r], 32 * 16 + 32)

            @block.vector
            def _(dve):
                dve.sem_inc(tile_done, 2)
                def split_tile(pos, s):
                    t = 2 * pos + s
                    dve.wait_ge(w_loaded, 16 * t + 16)
                    dve.wait_ge(tile_done, t + 1)
                    nc.vector.tensor_copy(w_hi[:, s], raw[:]).then_inc(hi_split, 1)
                    dve.wait_ge(hi_split, t + 1)
                    nc.vector.tensor_tensor(w_lo[:, s], raw[:], w_hi[:, s].bitcast(F32), ALU.subtract).then_inc(split, 1)

                split_tile(0, 0)
                split_tile(0, 1)
                dve.wait_ge(consts, 48)

                def shuffle(kind, pos, i):
                    q = 8 * (pos - ROT0) + i
                    dve.wait_ge(copied, 8 * pos + i + 1 + 8)
                    dve.wait_ge(added, q + 1 - 2 + C_ADDED)
                    dve.sem_inc(waited, 1)
                    nc.vector.stream_shuffle(swap[:, i % 2, :], rows[:, i % NR, :], SWAP[kind]).then_inc(shuffled, 1)

                def add(pos, i):
                    q = 8 * (pos - ROT0) + i
                    dve.wait_ge(scaled, q + 1)
                    nc.vector.tensor_tensor(rows[:, i % NR, :], rows[:, i % NR, :], swap[:, i % 2, :], ALU.add).then_inc(added, 1)

                def lows(pos, i):
                    a = 8 * (pos - ATT0) + i
                    dve.wait_ge(hi_done, a + 1)
                    nc.vector.tensor_tensor(lo[:, i % 2, :], rows[:, i % NR, :], hi[:, i % 2, :].bitcast(F32), ALU.subtract).then_inc(lo_done, 1)
                    dve.wait_ge(lo_done, a + 1)
                    dve.sem_inc(row_free[i % NR], 16)

                for kind, first, end, shift in sections():
                    rotated = kind in ("ret", "att")

                    def body(pair):
                        pos = pair + shift
                        for s in range(2):
                            if rotated:
                                for g in range(GROUPS):
                                    i = s * GROUPS + g
                                    shuffle(kind, pos, i)
                                    if g:
                                        add(pos, i - 1)
                                    if g > 1 and kind == "att":
                                        lows(pos, i - 2)
                                add(pos, i)
                                if kind == "att":
                                    lows(pos, i - 1)
                                    lows(pos, i)
                            split_tile(pos + 1, s)

                    closing = shift + end == pairs
                    with dve.Fori(first, end - 1 if closing else end) as pair:
                        body(pair)

            @block.tensor
            def _(pe):
                pe.sem_inc(copied, 2 * GROUPS)
                with pe.Fori(0, pairs) as pos:
                    for s in range(2):
                        pe.wait_ge(split, 2 * pos + s + 1)
                        for g in range(GROUPS):
                            pe.wait_ge(copied, 8 * pos + s * GROUPS + g + 1)
                            t = slice(g * GROUP, (g + 1) * GROUP)
                            n = 0
                            for k in range(KT):
                                for w, h in ((w_hi, hT_hi), (w_hi, hT_lo), (w_lo, hT_hi)):
                                    last = nc.tensor.matmul(acc[:, s, g, :], w[:, s, k, :], h[:, k, t],
                                                            start=n == 0, stop=n == 3 * KT - 1)
                                    n += 1
                            last.then_inc(group_done, 1)
                        pe.wait_ge(group_done, 8 * pos + (s + 1) * GROUPS)
                        pe.sem_inc(tile_done, 1)

            @block.scalar
            def _(act):
                for r in range(NR):
                    act.sem_inc(row_free[r], 16)
                for r in range(2):
                    act.sem_inc(parts_stored[r], 32)
                act.sem_inc(added, C_ADDED)
                for kind, first, end, shift in sections():
                    if kind == "ret":
                        for n, (of, c) in enumerate((("ret", 2), ("att", 0))):
                            cosT, sinT = table[of]
                            act.wait_ge(angles[n], 1)
                            nc.scalar.activation(sinT[:], cosT[:], ACT.Sin, scale=rotation[:, c + 1:c + 2]).then_inc(tables_done, 1)
                            act.wait_ge(tables_done, 3 * n + 1)
                            nc.scalar.activation(cosT[:], cosT[:], ACT.Abs).then_inc(tables_done, 1)
                            act.wait_ge(tables_done, 3 * n + 2)
                            nc.scalar.activation(cosT[:], cosT[:], ACT.Sin, bias=quarter[:], scale=-1.0).then_inc(tables_done, 1)

                    def high(pos, i):
                        a = 8 * (pos - ATT0) + i
                        act.wait_ge(added, a + 8 * (ATT0 - ROT0) + 1 + C_ADDED)
                        act.wait_ge(parts_stored[i % 2], 32 * 4 * (pos - ATT0) + 32 * (i // 2) + 32)
                        nc.scalar.activation(hi[:, i % 2, :], rows[:, i % NR, :], ACT.Copy).then_inc(hi_done, 1)

                    with act.Fori(first, end) as pair:
                        pos = pair + shift
                        for i in range(8):
                            act.wait_ge(row_free[i % NR], 32 * pos + 16 * (i // NR) + 16)
                            act.wait_ge(group_done, 8 * pos + i + 1)
                            nc.scalar.activation(rows[:, i % NR, :], acc[:, i // GROUPS, i % GROUPS, :],
                                                 ACT.Silu if kind == "silu" else ACT.Copy).then_inc(copied, 1)
                            if kind == "att" and i % GROUPS:
                                high(pos, i - 1)
                            if kind == "att" and i % GROUPS == GROUPS - 1:
                                high(pos, i)

            @block.gpsimd
            def _(pool):
                step = [0]

                def then(instruction):
                    step[0] += 1
                    instruction.then_inc(angle_step, 1)
                    pool.wait_ge(angle_step, step[0])

                MAGIC = 1.5 * 2.0 ** 23
                pool.wait_ge(consts, 48)
                then(nc.gpsimd.memset(quarter[:], math.pi / 2))
                for n, (kind, c) in enumerate((("ret", 2), ("att", 0))):
                    angle, turns = table[kind]
                    then(nc.gpsimd.tensor_copy(angle[:], turns[:].bitcast(I32)))
                    then(nc.gpsimd.tensor_scalar(angle[:], angle[:], rotation[:, c:c + 1], None, ALU.mult))
                    then(nc.gpsimd.tensor_scalar(turns[:], angle[:], 1 / (2 * math.pi), MAGIC, ALU.mult, ALU.add))
                    then(nc.gpsimd.tensor_scalar(turns[:], turns[:], -MAGIC, None, ALU.add))
                    for half in range(2):
                        h = slice(half * SEQ // 2, (half + 1) * SEQ // 2)
                        for value in turns_parts():
                            then(nc.gpsimd.tensor_scalar(part[:], turns[:, h], value, None, ALU.mult))
                            then(nc.gpsimd.tensor_tensor(angle[:, h], angle[:, h], part[:], ALU.subtract))
                    then(nc.gpsimd.tensor_scalar(angle[:], angle[:], 3.1415925, -3.1415925, ALU.min, ALU.max))
                    pool.sem_inc(angles[n], 1)
                pool.wait_ge(tables_done, 6)
                for kind, first, end, shift in sections():
                    if kind not in ("ret", "att"):
                        continue
                    cosT, sinT = table[kind]
                    with pool.Fori(first, end) as pair:
                        for i in range(8):
                            q = 8 * (pair + shift - ROT0) + i
                            t = slice(i % GROUPS * GROUP, (i % GROUPS + 1) * GROUP)
                            pool.wait_ge(shuffled, q + 1)
                            nc.gpsimd.tensor_tensor(swap[:, i % 2, :], swap[:, i % 2, :], sinT[:, t], ALU.mult).then_inc(scaled0, 1)
                            pool.wait_ge(scaled0, q + 1)
                            nc.gpsimd.tensor_tensor(rows[:, i % NR, :], rows[:, i % NR, :], cosT[:, t], ALU.mult).then_inc(scaled, 1)


def attention_blocks():
    out = []
    for p, d in enumerate(PATTERNS):
        for r in range(d):
            for n in range(CHUNKS // d):
                out.append((p, r + d * P * n, d, n > 0))
    return out


def attention(nc, D, w_out):
    blocks = attention_blocks()
    NB = len(blocks)
    NU = ATT_HEADS // 2
    NV = NB // 4
    SCALE = ATT_D ** -0.5
    NS, AHEAD = 3, 4
    RING = 8
    with ExitStack() as ctx:
        m = Mem(nc, ctx, "at")
        ident = m.sb("ident", [P, P])
        mask = m.sb("mask", [P, 2 * P])
        q2 = m.sb("q2", [P, 2, 2, SEQ], F32R)
        k_hi2 = m.sb("k_hi2", [P, 2, 2, SEQ], F32R)
        k_lo2 = m.sb("k_lo2", [P, 2, 2, SEQ], F32R)
        vT = m.sb("vT", [P, 2, SEQ])
        vblk = m.sb("vblk", [P, NB, P])
        prob = m.sb("prob", [P, 4, 2, 2 * P])
        probT = m.sb("probT", [P, 2, 2, 2, P])
        bias = m.sb("bias", [P, 4, 2])
        orow = m.sb("orow", [P, RING, AO_W])
        s_ps = m.ps("s", [P, NS, 2, 2 * P])
        t_ps = m.ps("t", [P, 2, 2, 2, P])
        o_ps = m.ps("o", [P, 2, 2, 2 * P])
        v_ps = m.ps("v", [P, 4, P])
        consts = m.sem("consts")
        qk_first, qk_rest, v_loaded = m.sems("qk_first", 2), m.sems("qk_rest", 2), m.sems("v_loaded", 2)
        scored, maxed, biased, exped = m.sem("scored"), m.sem("maxed"), m.sem("biased"), m.sem("exped")
        turned = m.sem("turned")
        turn_copied = m.sems("turn_copied", 2)
        valued, o_copied = m.sem("valued"), m.sem("o_copied")
        waited = m.sem("waited")
        v_turned, v_copied = m.sem("v_turned"), m.sem("v_copied")
        stored = m.sems("stored", RING)
        C_MAXED, C_TURNED, C_COPIED, C_VALUED, C_O, C_V = NS, 4, 1, 2, 2, 1
        C_SCORED = 1
        keys = [slice(0, 2 * P) if b[3] else slice(P, 2 * P) for b in blocks]
        QK_DMAS = 12

        with nc.Block() as block:

            @block.sync
            def _(sp):
                sp.dma_start(ident[:], D["ident"]).then_inc(consts, 16)
                sp.dma_start(mask[:], D["mask"]).then_inc(consts, 16)

                def load_qk(u, s, n):
                    t, loaded = ((slice(0, GROUP), qk_first), (slice(GROUP, SEQ), qk_rest))[n // QK_DMAS]
                    h, tensor, lower = n % QK_DMAS // 6, n % 6 // 2, n % 2
                    tile, parts = ((q2, ("rot_hi", "rot_lo")), (k_hi2, ("rot_hi", "rot_hi")), (k_lo2, ("rot_lo", "rot_lo")))[tensor]
                    rows = bass.ds((u * P + h * ATT_D) + (WIDTH if tensor else 0), ATT_D)
                    sp.dma_start(tile[lower * ATT_D:(lower + 1) * ATT_D, s, h, t].bitcast(F32),
                                 D[parts[lower]][rows, t]).then_inc(loaded[s], 16)

                def load_v(u, s):
                    sp.dma_start(vT[:, s, :], D["projT"][AV:AV + WIDTH, :][bass.ts(u, P), :]).then_inc(v_loaded[s], 16)

                def store(u, j):
                    p, t0, d, _ = blocks[j]
                    sp.wait_ge(o_copied, NB * u + j + 1 + C_O)
                    dst = D["att_out"][p, t0:t0 + d * (P - 1) + 1:d, :]
                    sp.dma_start(dst[:, bass.ds(u * AO_W, AO_W)], orow[:, j % RING, :]).then_inc(stored[j % RING], 16)

                def unit(u, s, more=True):
                    if more:
                        sp.wait_ge(scored, NB * u + C_SCORED)
                        load_v(u + 1, 1 - s)
                    for j in range(NB):
                        store(u, j)
                        if more and j < 2 * QK_DMAS:
                            load_qk(u + 1, 1 - s, j)

                for n in range(QK_DMAS):
                    load_qk(0, 0, n)
                load_v(0, 0)
                for n in range(QK_DMAS, 2 * QK_DMAS):
                    load_qk(0, 0, n)
                with sp.Fori(0, NU // 2 - 1) as it:
                    unit(2 * it, 0)
                    unit(2 * it + 1, 1)
                unit(NU - 2, 0)
                sp.dma_start(w_out[:], D["w_out"].rearrange("(k p) n -> p k n", p=P)).then_inc(consts, 16)
                unit(NU - 1, 1, more=False)
                for r in range(RING):
                    sp.wait_ge(stored[r], 16 * (NU * NB // RING) + 16)
                sp.wait_ge(consts, 48)

            @block.tensor
            def _(pe):
                pe.sem_inc(scored, C_SCORED)
                pe.wait_ge(consts, 32)

                def transpose_values(it, u, s, gi):
                    if gi == 0:
                        pe.wait_ge(v_loaded[s], 16 * it + 16)
                    pe.wait_ge(v_copied, NV * u + gi + 1)
                    for b in range(4):
                        _, t0, d, _ = blocks[4 * gi + b]
                        last = nc.tensor.transpose(v_ps[:, b, :], vT[:, s, t0:t0 + d * (P - 1) + 1:d], ident[:])
                    last.then_inc(v_turned, 1)

                def scores(it, u, s, j):
                    _, t0, d, before = blocks[j]
                    k0 = t0 - d * P if before else t0
                    nk = 2 * P if before else P
                    if j == 0:
                        pe.wait_ge(qk_first[s], 16 * QK_DMAS * it + 16 * QK_DMAS)
                    if j == GROUP // P:
                        pe.wait_ge(qk_rest[s], 16 * QK_DMAS * it + 16 * QK_DMAS)
                    pe.wait_ge(maxed, NB * u + j + 1)
                    for h in range(2):
                        q = q2[:, s, h, t0:t0 + d * (P - 1) + 1:d]
                        for k in (k_hi2, k_lo2):
                            last = nc.tensor.matmul(s_ps[:, j % NS, h, keys[j]], q, k[:, s, h, k0:k0 + d * (nk - 1) + 1:d],
                                                    start=k is k_hi2, stop=k is k_lo2)
                    last.then_inc(scored, 1)

                def turn(u, j):
                    pe.wait_ge(exped, NB * u + j + 1)
                    pe.wait_ge(turn_copied[j % 2], (NB // 2) * u + j // 2 + 1)
                    for h in range(2):
                        for kb in range(2):
                            if kb == 1 or blocks[j][3]:
                                last = nc.tensor.transpose(t_ps[:, j % 2, h, kb, :], prob[:, j % 4, h, kb * P:(kb + 1) * P], ident[:])
                    last.then_inc(turned, 1)

                def values(u, j):
                    if j % 4 == 0:
                        pe.wait_ge(v_copied, NV * u + j // 4 + 1 + C_V)
                    pe.wait_ge(turn_copied[j % 2], (NB // 2) * u + j // 2 + 1 + C_COPIED)
                    pe.wait_ge(o_copied, NB * u + j + 1)
                    first = 0 if blocks[j][3] else 1
                    for h in range(2):
                        out = o_ps[:, j % 2].rearrange("p a b -> p (a b)")[:, h * (2 * P - ATT_D):h * (2 * P - ATT_D) + P]
                        for kb in range(first, 2):
                            last = nc.tensor.matmul(out, probT[:, j % 2, h, kb, :], vblk[:, j - 1 + kb, :],
                                                    start=kb == first, stop=kb == 1)
                    last.then_inc(valued, 1)

                with pe.Fori(0, NU // 2) as it:
                    def at(J):
                        return 2 * it + J // NB, J // NB, J % NB

                    transpose_values(it, 2 * it, 0, 0)
                    for J in range(AHEAD):
                        scores(it, *at(J))
                    turn(2 * it, 0)
                    for J in range(2 * NB):
                        u, s, j = at(J)
                        if j % 4 == 0 and j // 4 + 1 < NV:
                            transpose_values(it, u, s, j // 4 + 1)
                        if J == NB - 1:
                            transpose_values(it, u + 1, 1, 0)
                        if j == NB - 1:
                            values(u, j)
                        if J + AHEAD < 2 * NB:
                            scores(it, *at(J + AHEAD))
                        if J + 1 < 2 * NB:
                            un, _, jn = at(J + 1)
                            turn(un, jn)
                        if j < NB - 1:
                            values(u, j)

            @block.vector
            def _(dve):
                dve.sem_inc(maxed, C_MAXED)
                dve.sem_inc(turn_copied[0], C_COPIED)
                dve.sem_inc(v_copied, C_V)
                dve.sem_inc(turned, C_TURNED)
                for r in range(RING):
                    dve.sem_inc(stored[r], 16)
                dve.wait_ge(consts, 32)

                def copy_values(u, gi):
                    dve.wait_ge(v_turned, NV * u + gi + 1)
                    nc.vector.tensor_copy(vblk[:, 4 * gi:4 * gi + 4, :], v_ps[:]).then_inc(v_copied, 1)

                def copy_turned(u, j):
                    dve.wait_ge(valued, NB * u + j + 1)
                    dve.wait_ge(turned, NB * u + j + 1 + C_TURNED)
                    kb = 0 if blocks[j][3] else 1
                    nc.vector.tensor_copy(probT[:, 0, :, kb:, :], t_ps[:, 0, :, kb:, :]).then_inc(turn_copied[0], 1)

                with dve.Fori(0, NU) as u:
                    copy_values(u, 0)
                    for j in range(NB):
                        dve.wait_ge(scored, NB * u + j + 1 + C_SCORED)
                        dve.wait_ge(turned, NB * u + j + 1)
                        dve.wait_ge(stored[j % RING], 16 * (NB // RING) * u + 16 * (j // RING) + 16)
                        dve.sem_inc(waited, 1)
                        for h in range(2):
                            last = nc.vector.tensor_tensor_reduce(
                                out=prob[:, j % 4, h, keys[j]], in0=s_ps[:, j % NS, h, keys[j]], in1=mask[:, keys[j]],
                                scale=1.0, scalar=3 * NEG, op0=ALU.add, op1=ALU.max,
                                accum_out=orow[:, j % RING, 2 * ATT_D + h:2 * ATT_D + h + 1])
                        last.then_inc(maxed, 1)
                        dve.wait_ge(maxed, NB * u + j + 1 + C_MAXED)
                        nc.vector.tensor_scalar(bias[:, j % 4, :], orow[:, j % RING, 2 * ATT_D:2 * ATT_D + 2], -SCALE, None,
                                                ALU.mult).then_inc(biased, 1)
                        if j >= 2 and j % 2 == 0:
                            copy_turned(u, j - 2)
                        if j >= 3 and (j - 3) % 4 == 0 and (j - 3) // 4 + 1 < NV:
                            copy_values(u, (j - 3) // 4 + 1)
                    copy_turned(u, NB - 2)

            @block.gpsimd
            def _(pool):
                pass

            @block.scalar
            def _(act):
                act.sem_inc(turn_copied[1], C_COPIED)
                act.sem_inc(valued, C_VALUED)
                act.sem_inc(o_copied, C_O)

                def copy_turned(u, j):
                    act.wait_ge(valued, NB * u + j + 1)
                    act.wait_ge(turned, NB * u + j + 1 + C_TURNED)
                    kb = 0 if blocks[j][3] else 1
                    nc.scalar.activation(probT[:, 1, :, kb:, :], t_ps[:, 1, :, kb:, :], ACT.Copy).then_inc(turn_copied[1], 1)

                def copy_out(u, j):
                    act.wait_ge(valued, NB * u + j + 1 + C_VALUED)
                    nc.scalar.activation(orow[:, j % RING, 0:2 * ATT_D].rearrange("p (h c) -> p h c", h=2), o_ps[:, j % 2, :, 0:ATT_D], ACT.Copy).then_inc(o_copied, 1)

                with act.Fori(0, NU) as u:
                    for j in range(NB):
                        act.wait_ge(biased, NB * u + j + 1)
                        for h in range(2):
                            pr = prob[:, j % 4, h, keys[j]]
                            last = nc.scalar.activation(pr, pr, ACT.Exp, bias=bias[:, j % 4, h:h + 1], scale=SCALE,
                                                        accum_out=orow[:, j % RING, 2 * ATT_D + 2 + h:2 * ATT_D + 3 + h])
                        last.then_inc(exped, 1)
                        if j >= 2 and j % 2 == 1:
                            copy_turned(u, j - 2)
                        if j >= 3:
                            copy_out(u, j - 3)
                    copy_turned(u, NB - 1)
                    for j in range(NB - 3, NB):
                        copy_out(u, j)


def mix(nc, D, w_out):
    NU = 2
    HU = RET_HEADS // NU
    SCALE = ATT_D ** -0.5
    QW = ATT_HEADS // 2 * AO_W
    with ExitStack() as ctx:
        m = Mem(nc, ctx, "mx")
        w_hi = m.sb("w_hi", [P, KT, DM], F32R)
        w_lo = m.sb("w_lo", [P, KT, DM], F32R)
        ident = m.sb("ident", [P, P])
        k_decay = m.sb("k_decay", [P, NU, P])
        q_decay = m.sb("q_decay", [P, NU, P])
        decay = m.sb("decay", [P, NU, HU, P])
        head_rows = m.sb("head_rows", [P, HU])
        head_cols = m.sb("head_cols", [P, HU * RET_DV])
        chunk_decay = m.sb("chunk_decay", [P, NU])
        gain_mix = m.sb("gain_mix", [P, DM])
        gain_ffn = m.sb("gain_ffn", [P, DM])
        minus_half = m.sb("minus_half", [P, RET_HEADS])
        qkv = m.sb("qkv", [P, 2, 8, P])
        q_heads = m.sb("q_heads", [P, NU, HU, P])
        q_dec = m.sb("q_dec", [P, NU, P])
        k_dec = m.sb("k_dec", [P, NU, P])
        v_pad = m.sb("v_pad", [P, 2, RET_HEADS, P])
        probT = m.sb("probT", [P, NU, HU, P])
        kv = m.sb("kv", [P, NU, HU * RET_DV])
        state = m.sb("state", [P, 2, NU, HU * RET_DV])
        stat = m.sb("stat", [P, 4, RET_HEADS])
        centred = m.sb("centred", [P, RET_HEADS, RET_DV])
        squares = m.sb("squares", [P, RET_HEADS, RET_DV])
        ret = m.sb("ret", [P, WIDTH])
        att_in = m.sb("att_in", [P, 2, 3, QW])
        gate = m.sb("gate", [P, 2, 4, P])
        att_max = m.sb("att_max", [P, 8])
        weight = m.sb("weight", [P, 3, 8])
        scaled_sum = m.sb("scaled_sum", [P, 3, 8])
        sum8 = m.sb("sum8", [P, 8])
        parts = m.sb("parts", [P, 2, 3, 8, ATT_D])
        mixT = m.sb("mixT", [P, 4, P])
        mT_hi = m.sb("mT_hi", [P, 2, KT, P], F32R)
        mT_lo = m.sb("mT_lo", [P, 2, KT, P], F32R)
        xin, row_squares, x1, h2 = w_out[:, 0:2, :], w_out[:, 2:4, :], w_out[:, 4, :], w_out[:, 5, :]
        ssq = m.sb("ssq", [P, 4])
        hT_hi = m.sb("hT_hi", [P, KT, P], F32R)
        hT_lo = m.sb("hT_lo", [P, KT, P], F32R)
        tp = m.ps("tp", [P, KT, P])
        s_ps = m.ps("s", [P, NU, HU, P])
        o_ps = m.ps("o", [P, RET_HEADS, RET_DV])
        kv_ps = m.ps("kv", [P, NU, HU * RET_DV])
        y_ps = m.ps("y", [P, 2, GROUP])

        names = ("waited consts w_split w_hi_split zeroed turned k_done v_done q_ready q_dec_ready "
                 "scored prob_done output kv_done kv_masked state_done summed meaned centre_done squared var_sum var_done "
                 "rooted ret_done maxed differed exped dens_done sum_done recip_done weighted parted parts_a att_done "
                 "mix_turned gated hi_a hi_b lo_a lo_b y0_done y_done y_sq y_mean y_root y_scaled x1_done half_set x_sq x_mean x_root "
                 "h2_done h_turned h_hi h_lo").split()
        S = {n: m.sem(n) for n in names}
        qkv_loaded, att_loaded = m.sems("qkv_loaded", 2), m.sems("att_loaded", 2)
        x_loaded = m.sems("x_loaded", 2)
        x1_stored, h_stored = m.sem("x1_stored"), m.sem("h_stored")
        ident_loaded, late_consts = m.sem("ident_loaded"), m.sem("late_consts")
        CONSTS = 4

        LAG_MIX, LAG_OUT, LAG_H = 1, 2, 3
        FIRST, LAST = LAG_H + 1, CHUNKS - 2

        def steps(eng, step):
            for c in range(FIRST):
                step(c, c % 2, lambda lag, c=c: 0 <= c - lag < CHUNKS)
            with eng.Fori(0, (LAST - FIRST) // 2) as it:
                for s in range(2):
                    step(2 * it + (FIRST + s), s, lambda lag: True)
            for c in range(LAST, CHUNKS + LAG_H):
                step(c, c % 2, lambda lag, c=c: 0 <= c - lag < CHUNKS)

        def later(d):
            return not isinstance(d, int) or d > 0

        def wait_loaded(eng, sem, c, s, each):
            if isinstance(c, int):
                eng.wait_ge(sem, 16 * each * (c // 2 + 1))
            else:
                eng.wait_ge(sem, 8 * each * (c - s) + 16 * each)

        with nc.Block() as block:

            @block.sync
            def _(sp):
                def taken():
                    sp.sem_inc(S["waited"], 1)

                def load_ret(c, s):
                    for n, (at, base, tiles) in enumerate(((0, RQ, 2), (2, RK, 2), (4, RV, 4))):
                        src = D["projT"][base:base + tiles * P, bass.ts(c, P)].rearrange("(k p) t -> p k t", p=P)
                        sp.dma_start(qkv[:, s, at:at + tiles, :], src).then_inc(qkv_loaded[s], 16)

                def load_att(c, s):
                    src = D["att_out"][:, bass.ts(c, P), :].rearrange("a t n -> t a n")
                    sp.dma_start(att_in[:, s], src).then_inc(att_loaded[s], 16)
                    src = D["projT"][RG:RG + WIDTH, bass.ts(c, P)].rearrange("(k p) t -> p k t", p=P)
                    sp.dma_start(gate[:, s], src).then_inc(att_loaded[s], 16)

                sp.dma_start(ident[:], D["ident"]).then_inc(ident_loaded, 16)
                load_ret(0, 0)
                for tile, name in ((head_rows, "head_rows"), (q_decay, "q_decay"), (k_decay, "k_decay"), (decay, "decay")):
                    sp.dma_start(tile[:], D[name]).then_inc(S["consts"], 16)
                load_att(0, 0)
                for tile, name in ((head_cols, "head_cols"), (chunk_decay, "chunk_decay")):
                    sp.dma_start(tile[:], D[name]).then_inc(late_consts, 16)
                sp.dma_start(gain_mix[:], D["g_post_mix"].broadcast_to([P, DM])).then_inc(late_consts, 16)
                sp.dma_start(gain_ffn[:], D["g_pre_ffn"].broadcast_to([P, DM])).then_inc(late_consts, 16)

                def step(c, s, on):
                    more = on(0) and (not isinstance(c, int) or c + 1 < CHUNKS)
                    if more:
                        if later(c):
                            sp.wait_ge(S["output"], 2 * c)
                            taken()
                        load_ret(c + 1, 1 - s)
                    if on(LAG_H):
                        d = c - LAG_H
                        sp.wait_ge(S["x1_done"], d + 1)
                        taken()
                        sp.dma_start(D["x1"][bass.ts(d, P), :], x1[:]).then_inc(x1_stored, 16)
                    if on(LAG_OUT):
                        if isinstance(c, int) and c == LAG_OUT:
                            sp.wait_ge(S["w_split"], KT)
                        sp.dma_start(xin[:, s], D["x"][bass.ts(c - LAG_OUT, P), :]).then_inc(x_loaded[s], 16)
                    if more:
                        if later(c):
                            sp.wait_ge(S["gated"], c)
                            taken()
                            sp.wait_ge(S["parted"], 3 * c)
                            taken()
                        load_att(c + 1, 1 - s)
                    if on(LAG_H):
                        d = c - LAG_H
                        sp.wait_ge(S["h_lo"], d + 1)
                        taken()
                        for tile, name in ((hT_hi, "h_hi"), (hT_lo, "h_lo")):
                            dst = D[name][:, bass.ts(d, P)].rearrange("(k p) t -> p k t", p=P)
                            sp.dma_start(dst, tile[:].bitcast(F32)).then_inc(h_stored, 16)

                steps(sp, step)
                sp.wait_ge(h_stored, 32 * CHUNKS)
                sp.wait_ge(x1_stored, 16 * CHUNKS)

            @block.tensor
            def _(pe):
                pe.wait_ge(ident_loaded, 16)

                def step(c, s, on):
                    if on(0):
                        wait_loaded(pe, qkv_loaded[s], c, s, 3)
                        if later(c):
                            if on(LAG_H + 1):
                                pe.wait_ge(S["h_lo"], c - LAG_H)
                            elif on(LAG_MIX + 1):
                                pe.wait_ge(S["lo_b"], c - 1)
                            else:
                                pe.wait_ge(S["k_done"], c)
                                pe.wait_ge(S["v_done"], c)
                        for to, of in enumerate((4, 5, 6, 7, 2, 3)):
                            last = nc.tensor.transpose(tp[:, to, :], qkv[:, s, of, :], ident[:])
                        last.then_inc(S["turned"], 1)
                        for u in range(NU):
                            pe.wait_ge(S["q_ready"], 2 * c + u + 1)
                            if later(c):
                                pe.wait_ge(S["prob_done"], 2 * c + u - 1)
                            nc.tensor.matmul(s_ps[:, u], qkv[:, s, 2 + u, :], q_heads[:, u], start=True, stop=True).then_inc(S["scored"], 1)
                    if on(LAG_OUT):
                        d = c - LAG_OUT
                        if isinstance(c, int) and d == 0:
                            pe.wait_ge(S["w_split"], KT)
                        pe.wait_ge(S["lo_b"], d + 1)
                        if later(d):
                            pe.wait_ge(S["y_scaled"], 2 * d - 1)
                        out_half(0, s).then_inc(S["y0_done"], 1)
                    if on(LAG_MIX):
                        d = c - LAG_MIX
                        pe.wait_ge(S["ret_done"], d + 1)
                        pe.wait_ge(S["att_done"], d + 1)
                        if on(0):
                            pe.wait_ge(S["k_done"], c + 1)
                            pe.wait_ge(S["v_done"], c + 1)
                        else:
                            pe.wait_ge(S["h_lo"], c - LAG_H)
                        for i in range(4):
                            nc.tensor.transpose(tp[:, i, :], ret[:, i * P:(i + 1) * P], ident[:])
                        for i in range(4):
                            last = nc.tensor.transpose(tp[:, 4 + i, :], parts[:, 1 - s, 0, 2 * i:2 * i + 2, :], ident[:])
                        last.then_inc(S["mix_turned"], 1)
                    if on(0):
                        first = not later(c)
                        for u in range(NU):
                            pe.wait_ge(S["prob_done"], 2 * c + u + 1)
                            if u == 0:
                                pe.wait_ge(S["v_done"], c + 1)
                                pe.wait_ge(S["q_dec_ready"], c + 1)
                                if first:
                                    pe.wait_ge(S["zeroed"], 3)
                                else:
                                    pe.wait_ge(S["centre_done"], c)
                                    pe.wait_ge(S["state_done"], 2 * c)
                            flat = o_ps[:].rearrange("p h e -> p (h e)")
                            at = u * HU * RET_DV
                            nc.tensor.matmul(flat[:, at:at + HU * RET_DV], q_dec[:, u, :], state[:, s, u, :], start=u == 0, stop=False,
                                             skip_group_check=True)
                            for h in range(HU):
                                to = at + (h // 2) * P
                                of = (u * HU + h) * P - (h % 2) * RET_DV
                                v = v_pad[:, s].rearrange("p h e -> p (h e)")[:, of:of + P]
                                last = nc.tensor.matmul(flat[:, to:to + P], probT[:, u, h, :], v, start=False,
                                                        stop=u == NU - 1 and h == HU - 1, skip_group_check=True)
                            last.then_inc(S["output"], 1)
                        pe.wait_ge(S["k_done"], c + 1)
                        if not first:
                            pe.wait_ge(S["kv_masked"], c)
                        for u in range(NU):
                            v = v_pad[:, s, u * HU:(u + 1) * HU, 0:RET_DV]
                            last = nc.tensor.matmul(kv_ps[:, u, :], k_dec[:, u, :], v, start=u == 0, stop=u == NU - 1, skip_group_check=True)
                        last.then_inc(S["kv_done"], 1)
                    if on(LAG_H):
                        d = c - LAG_H
                        pe.wait_ge(S["h2_done"], d + 1)
                        if on(LAG_MIX):
                            pe.wait_ge(S["gated"], c)
                            pe.wait_ge(S["lo_a"], c)
                        else:
                            pe.wait_ge(S["h_lo"], d)
                        for i in range(KT):
                            last = nc.tensor.transpose(tp[:, i, :], h2[:, i * P:(i + 1) * P], ident[:])
                        last.then_inc(S["h_turned"], 1)
                    if on(LAG_OUT):
                        d = c - LAG_OUT
                        if later(d):
                            pe.wait_ge(S["y_scaled"], 2 * d)
                        out_half(1, s).then_inc(S["y_done"], 1)

                def out_half(half, s):
                    n = 0
                    for k in range(KT):
                        for a, w in ((mT_hi, w_hi), (mT_hi, w_lo), (mT_lo, w_hi)):
                            last = nc.tensor.matmul(y_ps[:, half, :], a[:, s, k, :], w[:, k, half * GROUP:(half + 1) * GROUP],
                                                    start=n == 0, stop=n == 3 * KT - 1)
                            n += 1
                    return last

                steps(pe, step)

            @block.vector
            def _(dve):
                for s in range(2):
                    nc.vector.memset(v_pad[:, s], 0.0).then_inc(S["zeroed"], 1)
                nc.vector.memset(state[:, 0], 0.0).then_inc(S["zeroed"], 1)
                dve.wait_ge(S["consts"], 16 * CONSTS)

                def split_w(ks):
                    for k in ks:
                        dve.wait_ge(S["w_hi_split"], k + 1)
                        nc.vector.tensor_tensor(w_lo[:, k, :], w_out[:, k, :], w_hi[:, k, :].bitcast(F32),
                                                ALU.subtract).then_inc(S["w_split"], 1)

                def step(c, s, on):
                    if on(LAG_H):
                        d = c - LAG_H
                        dve.wait_ge(S["y_sq"], 2 * d + 2)
                        nc.vector.scalar_tensor_tensor(ssq[:, 1:2], ssq[:, 0:1], RMS_EPS, ssq[:, 1:2], ALU.add, ALU.add).then_inc(S["y_mean"], 1)
                        dve.wait_ge(S["y_root"], d + 1)
                        if later(d):
                            dve.wait_ge(x1_stored, 16 * d)
                            dve.wait_ge(S["h2_done"], d)
                        for half in range(2):
                            cols = slice(half * GROUP, (half + 1) * GROUP)
                            nc.vector.scalar_tensor_tensor(x1[:, cols], y_ps[:, half, :], ssq[:, 1:2], gain_mix[:, cols],
                                                           ALU.mult, ALU.mult).then_inc(S["y_scaled"], 1)
                        dve.wait_ge(S["y_scaled"], 2 * d + 2)
                        wait_loaded(dve, x_loaded[1 - s], d, 1 - s, 1)
                        nc.vector.tensor_tensor(x1[:], x1[:], xin[:, 1 - s], ALU.add).then_inc(S["x1_done"], 1)
                    if on(0):
                        a = att_in[:, s].rearrange("p a (u n) -> p a u n", n=AO_W)
                        maxima, sums = a[:, :, :, 2 * ATT_D:2 * ATT_D + 2], a[:, :, :, 2 * ATT_D + 2:2 * ATT_D + 4]
                        four = lambda t: t.rearrange("p (u h) -> p u h", h=2)
                        wait_loaded(dve, att_loaded[s], c, s, 2)
                        nc.vector.tensor_tensor(four(att_max[:]), maxima[:, 0], maxima[:, 1], ALU.max).then_inc(S["maxed"], 1)
                        dve.wait_ge(S["maxed"], 2 * c + 1)
                        nc.vector.tensor_tensor(four(att_max[:]), four(att_max[:]), maxima[:, 2], ALU.max).then_inc(S["maxed"], 1)
                        dve.wait_ge(S["maxed"], 2 * c + 2)
                        if later(c):
                            dve.wait_ge(S["parted"], 3 * c)
                        for p in range(3):
                            last = nc.vector.tensor_tensor(four(weight[:, p, :]), maxima[:, p], four(att_max[:]), ALU.subtract)
                        last.then_inc(S["differed"], 1)
                        dve.wait_ge(S["turned"], c + 1)
                        if later(c):
                            dve.wait_ge(S["kv_done"], c)
                        nc.vector.tensor_tensor(k_dec[:], tp[:, 4:6, :], k_decay[:], ALU.mult).then_inc(S["k_done"], 1)
                        for u in range(NU):
                            dve.wait_ge(S["scored"], 2 * c + u + 1)
                            if later(c):
                                dve.wait_ge(S["output"], 2 * c + u - 1)
                            nc.vector.tensor_tensor(probT[:, u], s_ps[:, u], decay[:, u], ALU.mult).then_inc(S["prob_done"], 1)
                        dve.wait_ge(S["exped"], c + 1)
                        for p in range(3):
                            last = nc.vector.tensor_tensor(four(scaled_sum[:, p, :]), four(weight[:, p, :]), sums[:, p], ALU.mult)
                        last.then_inc(S["dens_done"], 1)
                        dve.wait_ge(S["dens_done"], c + 1)
                        nc.vector.tensor_reduce(sum8[:], scaled_sum[:].rearrange("p a h -> p h a"), AX.X, ALU.add).then_inc(S["sum_done"], 1)
                        dve.wait_ge(S["sum_done"], c + 1)
                        nc.vector.reciprocal(sum8[:], sum8[:]).then_inc(S["recip_done"], 1)
                        dve.wait_ge(S["recip_done"], c + 1)
                        for p in range(3):
                            last = nc.vector.tensor_tensor(weight[:, p, :], weight[:, p, :], sum8[:], ALU.mult)
                        last.then_inc(S["weighted"], 1)
                    if on(LAG_H):
                        d = c - LAG_H
                        dve.wait_ge(S["x_sq"], d + 1)
                        nc.vector.tensor_scalar(ssq[:, 3:4], ssq[:, 2:3], RMS_EPS, None, ALU.add).then_inc(S["x_mean"], 1)
                        dve.wait_ge(S["x_root"], d + 1)
                        if later(d):
                            dve.wait_ge(S["h_turned"], d)
                        nc.vector.scalar_tensor_tensor(h2[:], x1[:], ssq[:, 3:4], gain_ffn[:], ALU.mult, ALU.mult).then_inc(S["h2_done"], 1)
                    if on(LAG_MIX):
                        d = c - LAG_MIX
                        dve.wait_ge(S["mix_turned"], d + 1)
                        if later(d):
                            dve.wait_ge(S["hi_a"], d)
                            dve.wait_ge(S["lo_a"], d)
                        nc.vector.tensor_tensor(mixT[:], tp[:, 0:4, :], gate[:, 1 - s], ALU.mult).then_inc(S["gated"], 1)
                        dve.wait_ge(S["hi_b"], d + 1)
                        nc.vector.tensor_tensor(mT_lo[:, 1 - s, 4:8, :], tp[:, 4:8, :], mT_hi[:, 1 - s, 4:8, :].bitcast(F32),
                                                ALU.subtract).then_inc(S["lo_a"], 1)
                        dve.wait_ge(S["hi_a"], d + 1)
                        nc.vector.tensor_tensor(mT_lo[:, 1 - s, 0:4, :], mixT[:], mT_hi[:, 1 - s, 0:4, :].bitcast(F32),
                                                ALU.subtract).then_inc(S["lo_b"], 1)
                    if on(0):
                        dve.wait_ge(S["output"], 2 * c + 2)
                        nc.vector.tensor_reduce(stat[:, 0, :], o_ps[:], AX.X, ALU.add).then_inc(S["summed"], 1)
                        dve.wait_ge(S["summed"], c + 1)
                        nc.vector.tensor_scalar(stat[:, 1, :], stat[:, 0, :], 1.0 / RET_DV, None, ALU.mult).then_inc(S["meaned"], 1)
                        dve.wait_ge(S["meaned"], c + 1)
                        if later(c):
                            dve.wait_ge(S["ret_done"], c)
                        nc.vector.tensor_tensor(centred[:], o_ps[:], stat[:, 1, :].unsqueeze(2).broadcast_to([P, RET_HEADS, RET_DV]),
                                                ALU.subtract).then_inc(S["centre_done"], 1)
                        if not later(c):
                            dve.wait_ge(late_consts, 64)
                        dve.wait_ge(S["kv_done"], c + 1)
                        cols = head_cols[:].unsqueeze(1).broadcast_to([P, NU, HU * RET_DV])
                        nc.vector.tensor_tensor(kv[:], kv_ps[:], cols, ALU.mult).then_inc(S["kv_masked"], 1)
                        dve.wait_ge(S["kv_masked"], c + 1)
                        for u in range(NU):
                            nc.vector.scalar_tensor_tensor(state[:, 1 - s, u, :], state[:, s, u, :], chunk_decay[:, u:u + 1], kv[:, u, :],
                                                           ALU.mult, ALU.add).then_inc(S["state_done"], 1)
                        dve.wait_ge(S["squared"], c + 1)
                        nc.vector.tensor_reduce(stat[:, 2, :], squares[:], AX.X, ALU.add).then_inc(S["var_sum"], 1)
                        dve.wait_ge(S["var_sum"], c + 1)
                        nc.vector.tensor_scalar(stat[:, 2, :], stat[:, 2, :], 1.0 / RET_DV, GN_EPS, ALU.mult, ALU.add).then_inc(S["var_done"], 1)
                    if isinstance(c, int) and c < 2:
                        split_w(range(c * KT // 2, (c + 1) * KT // 2))
                    if on(LAG_H):
                        d = c - LAG_H
                        dve.wait_ge(S["h_hi"], d + 1)
                        nc.vector.tensor_tensor(hT_lo[:], tp[:], hT_hi[:].bitcast(F32), ALU.subtract).then_inc(S["h_lo"], 1)

                steps(dve, step)

            @block.scalar
            def _(act):
                ROOT = DM ** -0.5

                def step(c, s, on):
                    if on(LAG_H):
                        d = c - LAG_H
                        act.wait_ge(S["y_done"], d + 1)
                        nc.scalar.activation(row_squares[:, 0, GROUP:], y_ps[:, 1, :], ACT.Square, scale=ROOT,
                                             accum_out=ssq[:, 1:2]).then_inc(S["y_sq"], 1)
                    if on(0):
                        act.wait_ge(S["turned"], c + 1)
                        if not later(c):
                            act.wait_ge(S["zeroed"], 2)
                        v = tp[:, 0:4, :].rearrange("p k (h e) -> p (k h) e", e=RET_DV)
                        nc.scalar.activation(v_pad[:, s, :, 0:RET_DV], v, ACT.Copy).then_inc(S["v_done"], 1)
                        act.wait_ge(S["differed"], c + 1)
                        nc.scalar.activation(weight[:], weight[:], ACT.Exp, scale=SCALE).then_inc(S["exped"], 1)
                    if on(LAG_H):
                        act.wait_ge(S["x1_done"], d + 1)
                        nc.scalar.activation(row_squares[:, 1, :], x1[:], ACT.Square, scale=ROOT, accum_out=ssq[:, 2:3]).then_inc(S["x_sq"], 1)
                    if on(LAG_OUT):
                        d = c - LAG_OUT
                        act.wait_ge(S["y0_done"], d + 1)
                        if later(d):
                            act.wait_ge(S["y_mean"], d)
                        nc.scalar.activation(row_squares[:, 0, 0:GROUP], y_ps[:, 0, :], ACT.Square, scale=ROOT,
                                             accum_out=ssq[:, 0:1]).then_inc(S["y_sq"], 1)
                    if on(LAG_MIX):
                        d = c - LAG_MIX
                        act.wait_ge(S["mix_turned"], d + 1)
                        if not isinstance(c, int) or d > 1:
                            act.wait_ge(S["y_done"], d - 1)
                        nc.scalar.activation(mT_hi[:, 1 - s, 4:8, :], tp[:, 4:8, :], ACT.Copy).then_inc(S["hi_b"], 1)
                        act.wait_ge(S["gated"], d + 1)
                        nc.scalar.activation(mT_hi[:, 1 - s, 0:4, :], mixT[:], ACT.Copy).then_inc(S["hi_a"], 1)
                    if on(0):
                        act.wait_ge(S["centre_done"], c + 1)
                        nc.scalar.activation(squares[:], centred[:], ACT.Square).then_inc(S["squared"], 1)
                    if isinstance(c, int) and c < 2:
                        for k in range(c * KT // 2, (c + 1) * KT // 2):
                            nc.scalar.activation(w_hi[:, k, :], w_out[:, k, :], ACT.Copy).then_inc(S["w_hi_split"], 1)
                    if on(LAG_H):
                        d = c - LAG_H
                        act.wait_ge(S["h_turned"], d + 1)
                        if later(d):
                            act.wait_ge(h_stored, 32 * d)
                        nc.scalar.activation(hT_hi[:], tp[:], ACT.Copy).then_inc(S["h_hi"], 1)

                steps(act, step)

            @block.gpsimd
            def _(pool):
                nc.gpsimd.memset(minus_half[:], -0.5).then_inc(S["half_set"], 1)
                pool.wait_ge(S["half_set"], 1)
                pool.wait_ge(S["consts"], 16 * CONSTS)

                def queries(c, s):
                    wait_loaded(pool, qkv_loaded[s], c, s, 3)
                    if later(c):
                        pool.wait_ge(S["output"], 2 * c)
                    for u in range(NU):
                        q = qkv[:, s, u, :].unsqueeze(1).broadcast_to([P, HU, P])
                        rows = head_rows[:].unsqueeze(2).broadcast_to([P, HU, P])
                        nc.gpsimd.tensor_tensor(q_heads[:, u], q, rows, ALU.mult).then_inc(S["q_ready"], 1)
                    nc.gpsimd.tensor_tensor(q_dec[:], qkv[:, s, 0:NU, :], q_decay[:], ALU.mult).then_inc(S["q_dec_ready"], 1)

                def step(c, s, on):
                    if on(LAG_H):
                        d = c - LAG_H
                        pool.wait_ge(S["y_mean"], d + 1)
                        nc.gpsimd.tensor_tensor(ssq[:, 1:2], ssq[:, 1:2], minus_half[:, 0:1], ALU.pow).then_inc(S["y_root"], 1)
                        pool.wait_ge(S["x_mean"], d + 1)
                        nc.gpsimd.tensor_tensor(ssq[:, 3:4], ssq[:, 3:4], minus_half[:, 0:1], ALU.pow).then_inc(S["x_root"], 1)
                    if on(0):
                        pool.wait_ge(S["weighted"], c + 1)
                        if not isinstance(c, int) or c > 1:
                            pool.wait_ge(S["mix_turned"], c - 1)
                        for p in range(3):
                            four = lambda t: t.rearrange("p (u h) d -> p u h d", h=2)
                            part = att_in[:, s, p, :].rearrange("p (u n) -> p u n", n=AO_W)[:, :, 0:2 * ATT_D]
                            w = weight[:, p, :].rearrange("p (u h) -> p u h", h=2).unsqueeze(3).broadcast_to([P, 4, 2, ATT_D])
                            nc.gpsimd.tensor_tensor(four(parts[:, s, p]), part.rearrange("p u (h d) -> p u h d", h=2), w,
                                                    ALU.mult).then_inc(S["parted"], 1)
                        pool.wait_ge(S["parted"], 3 * c + 2)
                        nc.gpsimd.tensor_tensor(parts[:, s, 0], parts[:, s, 0], parts[:, s, 1], ALU.add).then_inc(S["parts_a"], 1)
                        pool.wait_ge(S["parts_a"], c + 1)
                        pool.wait_ge(S["parted"], 3 * c + 3)
                        nc.gpsimd.tensor_tensor(parts[:, s, 0], parts[:, s, 0], parts[:, s, 2], ALU.add).then_inc(S["att_done"], 1)
                        if not isinstance(c, int) or c + 1 < CHUNKS:
                            queries(c + 1, 1 - s)
                        pool.wait_ge(S["var_done"], c + 1)
                        nc.gpsimd.tensor_tensor(stat[:, 3, :], stat[:, 2, :], minus_half[:], ALU.pow).then_inc(S["rooted"], 1)
                        pool.wait_ge(S["rooted"], c + 1)
                        if later(c):
                            pool.wait_ge(S["mix_turned"], c)
                        r = stat[:, 3, :].unsqueeze(2).broadcast_to([P, RET_HEADS, RET_DV])
                        nc.gpsimd.tensor_tensor(ret[:].rearrange("p (h e) -> p h e", e=RET_DV), centred[:], r,
                                                ALU.mult).then_inc(S["ret_done"], 1)

                queries(0, 0)
                steps(pool, step)


def ffn(nc, D):
    TILES = 2
    PW = TILES * P
    PARTS = D_FF // PW
    HALVES = 2
    HALF = SEQ // HALVES
    UG = HALF // GROUP
    UC = GROUP // P
    with ExitStack() as ctx:
        m = Mem(nc, ctx, "ff")
        h_hi = m.sb("h_hi", [P, KT, HALF], F32R)
        h_lo = m.sb("h_lo", [P, KT, HALF], F32R)
        total = m.sb("total", [P, UG * UC, DM])
        raw = m.sb("raw", [P, 2, KT, PW])
        w_hi = m.sb("w_hi", [P, 2, KT, PW], F32R)
        w_lo = m.sb("w_lo", [P, 2, KT, PW], F32R)
        down_raw = m.sb("down_raw", [P, TILES, DM])
        down_hi = m.sb("down_hi", [P, TILES, DM], F32R)
        down_lo = m.sb("down_lo", [P, TILES, DM], F32R)
        gated = m.sb("gated", [P, TILES, GROUP])
        a_hi = m.sb("a_hi", [P, UG, TILES, GROUP], F32R)
        a_lo = m.sb("a_lo", [P, UG, TILES, GROUP], F32R)
        gain = m.sb("gain", [P, DM])
        x1 = m.sb("x1", [P, 2, DM])
        squares = m.sb("squares", [P, DM])
        ssq = m.sb("ssq", [P, UC])
        minus_half = m.sb("minus_half", [P, 1])
        gu_ps = m.ps("gu", [P, TILES, 2, GROUP])
        d_ps = m.ps("down", [P, 2, DM])
        gain_loaded, half_set = m.sem("gain_loaded"), m.sem("half_set")
        h_loaded = [m.sems(f"h_loaded{g}_", 2) for g in range(UG)]
        gu_loaded, down_loaded = m.sems("gu_loaded", 2), m.sem("down_loaded")
        gu_hi, gu_split, down_his, down_split = m.sem("gu_hi"), m.sem("gu_split"), m.sem("down_his"), m.sem("down_split")
        gu_done, silu_done, mul_done = m.sem("gu_done"), m.sem("silu_done"), m.sem("mul_done")
        a_hi_done, a_lo_done = m.sem("a_hi_done"), m.sem("a_lo_done")
        down_done, added = m.sem("down_done"), m.sem("added")
        squared, meaned, rooted = m.sem("squared"), m.sem("meaned"), m.sem("rooted")
        scaled, out_done = m.sem("scaled"), m.sem("out_done")
        x1_moved = m.sems("x1_moved", 2)
        B = 2

        def parts(eng, part):
            for half in range(HALVES):
                at = half * PARTS
                part(at, True, False, half)
                part(at + 1, False, False, half)
                with eng.Fori(at + 2, at + PARTS - 1) as J:
                    part(J, False, False, half)
                part(at + PARTS - 1, False, True, half)

        with nc.Block() as block:

            @block.sync
            def _(sp):
                def load_gu(j, which=(0, 1)):
                    for n in which:
                        src = D[("w_gate", "w_up")[n]][:, bass.ts(j, PW)].rearrange("(k p) n -> p k n", p=P)
                        sp.dma_start(raw[:, n], src).then_inc(gu_loaded[n], 16)

                def load_down(j):
                    sp.dma_start(down_raw[:], D["w_down"][bass.ts(j, PW), :].rearrange("(t p) n -> p t n", p=P)).then_inc(down_loaded, 16)

                def load_h(half, g, parts=(0, 1)):
                    t = slice(half * HALF + g * GROUP, half * HALF + (g + 1) * GROUP)
                    for part in parts:
                        k = slice(part * KT // 2, (part + 1) * KT // 2)
                        for tile, name in ((h_hi, "h_hi"), (h_lo, "h_lo")):
                            src = D[name][part * DM // 2:(part + 1) * DM // 2, t].rearrange("(k p) t -> p k t", p=P)
                            sp.dma_start(tile[:, k, g * GROUP:(g + 1) * GROUP].bitcast(F32), src).then_inc(h_loaded[g][part], 16)

                def load_x1(n):
                    if n >= 2:
                        sp.wait_ge(x1_moved[n % 2], 32 * (n // 2))
                    sp.dma_start(x1[:, n % 2], D["x1"][bass.ts(n, P), :]).then_inc(x1_moved[n % 2], 16)

                def finish(half, g):
                    for c in range(UC):
                        n = (half * UG + g) * UC + c
                        sp.wait_ge(out_done, n + 1)
                        sp.dma_start(D["out"][n * P:(n + 1) * P, :], x1[:, n % 2]).then_inc(x1_moved[n % 2], 16)
                        if n + 2 < HALVES * UG * UC:
                            load_x1(n + 2)

                load_gu(0, (0,))
                load_h(0, 0, (0,))
                load_gu(0, (1,))
                load_h(0, 0, (1,))
                sp.dma_start(gain[:], D["g_post_ffn"].broadcast_to([P, DM])).then_inc(gain_loaded, 16)
                load_down(0)
                load_h(0, 1)
                load_x1(0)
                load_x1(1)

                def part(J, first, last, half):
                    if not (last and half == HALVES - 1):
                        sp.wait_ge(gu_split, 4 * J + 4)
                        load_gu(0 if last else J + 1 - half * PARTS)
                    if first and half:
                        finish(half - 1, 1)
                    if last and half < HALVES - 1:
                        sp.wait_ge(gu_done, 8 * J + 4)
                        load_h(half + 1, 0)
                    if not (last and half == HALVES - 1):
                        sp.wait_ge(down_split, 2 * J + 2)
                        load_down(0 if last else J + 1 - half * PARTS)
                    if last:
                        if half < HALVES - 1:
                            sp.wait_ge(gu_done, 8 * J + 8)
                            load_h(half + 1, 1)
                        finish(half, 0)

                parts(sp, part)
                finish(HALVES - 1, 1)
                for s in range(2):
                    sp.wait_ge(x1_moved[s], 32 * HALVES * UG * UC // 2)

            @block.tensor
            def _(pe):
                pe.sem_inc(added, B)

                def gate_up(J, g, first, half):
                    u = 2 * J + g
                    t = slice(g * GROUP, (g + 1) * GROUP)
                    for tile in range(TILES):
                        cols = slice(tile * P, (tile + 1) * P)
                        for n, free in ((0, silu_done), (1, mul_done)):
                            if g == 0:
                                pe.wait_ge(gu_split, 4 * J + 2 * tile + n + 1)
                            if not (first and half == 0 and g == 0):
                                pe.wait_ge(free, 2 * u - 1 + tile)
                            i = 0
                            for k in range(KT):
                                if first and tile == n == 0 and k % (KT // 2) == 0:
                                    pe.wait_ge(h_loaded[g][2 * k // KT], 32 * (half + 1))
                                for w, h in ((w_hi, h_hi), (w_hi, h_lo), (w_lo, h_hi)):
                                    last = nc.tensor.matmul(gu_ps[:, tile, n], w[:, n, k, cols], h[:, k, t],
                                                            start=i == 0, stop=i == 3 * KT - 1)
                                    i += 1
                            last.then_inc(gu_done, 1)

                def down(J, g):
                    u = 2 * J + g
                    pe.wait_ge(a_hi_done, 2 * u + 2)
                    pe.wait_ge(a_lo_done, 2 * u + 2)
                    if g == 0:
                        pe.wait_ge(down_split, 2 * J + 2)
                    for c in range(UC):
                        pe.wait_ge(added, 4 * u + c - B + 1 + B)
                        for half in range(2):
                            i = 0
                            for tile in range(TILES):
                                for a, w in ((a_hi, down_hi), (a_hi, down_lo), (a_lo, down_hi)):
                                    last = nc.tensor.matmul(d_ps[:, c % 2, half * GROUP:(half + 1) * GROUP],
                                                            a[:, g, tile, c * P:(c + 1) * P],
                                                            w[:, tile, half * GROUP:(half + 1) * GROUP],
                                                            start=i == 0, stop=i == 3 * TILES - 1)
                                    i += 1
                        last.then_inc(down_done, 1)

                def part(J, first, last, half):
                    gate_up(J, 0, first, half)
                    if not (first and half == 0):
                        down(J - 1, 1)
                    gate_up(J, 1, first, half)
                    down(J, 0)

                parts(pe, part)
                down(HALVES * PARTS - 1, 1)

            @block.scalar
            def _(act):
                def split_gu(J, i):
                    tile, n = i // 2, i % 2
                    cols = slice(tile * P, (tile + 1) * P)
                    act.wait_ge(gu_loaded[n], 16 * J + 16)
                    if not (isinstance(J, int) and J == 0):
                        act.wait_ge(gu_done, 8 * J - 4 + i + 1)
                    nc.scalar.activation(w_hi[:, n, :, cols], raw[:, n, :, cols], ACT.Copy).then_inc(gu_hi, 1)

                def split_down(J):
                    act.wait_ge(down_loaded, 16 * J + 16)
                    if not (isinstance(J, int) and J == 0):
                        act.wait_ge(down_done, 8 * J)
                    for tile in range(TILES):
                        nc.scalar.activation(down_hi[:, tile], down_raw[:, tile], ACT.Copy).then_inc(down_his, 1)

                def products(J, g, tile):
                    u = 2 * J + g
                    act.wait_ge(gu_done, 4 * u + 2 * tile + 1)
                    if not (isinstance(u, int) and u == 0):
                        act.wait_ge(a_lo_done, 2 * u - 1 + tile)
                    nc.scalar.activation(gated[:, tile], gu_ps[:, tile, 0], ACT.Silu).then_inc(silu_done, 1)
                    act.wait_ge(mul_done, 2 * u + tile + 1)
                    nc.scalar.activation(a_hi[:, g, tile], gated[:, tile], ACT.Copy).then_inc(a_hi_done, 1)

                def finish(half, g):
                    for c in range(UC):
                        n = (half * UG + g) * UC + c
                        u = (half * PARTS + PARTS - 1) * UG + g
                        act.wait_ge(added, 4 * u + c + 1 + B)
                        if n:
                            act.wait_ge(squared, n)
                        if n >= UC:
                            act.wait_ge(scaled, n - UC + 1)
                        nc.scalar.activation(squares[:], total[:, g * UC + c], ACT.Square,
                                             accum_out=ssq[:, c:c + 1]).then_inc(squared, 1)

                for i in range(2 * TILES):
                    split_gu(0, i)

                def part(J, first, last, half):
                    for g in range(UG):
                        if g == 1:
                            split_down(J)
                        products(J, g, 0)
                        more = g == 1 and not (last and half == HALVES - 1)
                        if more:
                            split_gu(J + 1, 0)
                            split_gu(J + 1, 1)
                        products(J, g, 1)
                        if more:
                            split_gu(J + 1, 2)
                            split_gu(J + 1, 3)
                        if first and half and g == 0:
                            finish(half - 1, 1)
                        if last and g == 1:
                            finish(half, 0)

                parts(act, part)
                finish(HALVES - 1, 1)

            @block.gpsimd
            def _(pool):
                nc.gpsimd.memset(minus_half[:], -0.5).then_inc(half_set, 1)
                pool.wait_ge(half_set, 1)
                for n in range(HALVES * UG * UC):
                    c = slice(n % UC, n % UC + 1)
                    pool.wait_ge(meaned, n + 1)
                    nc.gpsimd.tensor_tensor(ssq[:, c], ssq[:, c], minus_half[:], ALU.pow).then_inc(rooted, 1)

            @block.vector
            def _(dve):
                def split_gu(J, i):
                    tile, n = i // 2, i % 2
                    cols = slice(tile * P, (tile + 1) * P)
                    dve.wait_ge(gu_hi, 4 * J + i + 1)
                    nc.vector.tensor_tensor(w_lo[:, n, :, cols], raw[:, n, :, cols], w_hi[:, n, :, cols].bitcast(F32),
                                            ALU.subtract).then_inc(gu_split, 1)

                def split_down(J):
                    for tile in range(TILES):
                        dve.wait_ge(down_his, 2 * J + tile + 1)
                        nc.vector.tensor_tensor(down_lo[:, tile], down_raw[:, tile], down_hi[:, tile].bitcast(F32),
                                                ALU.subtract).then_inc(down_split, 1)

                def products(J, g, tile):
                    u = 2 * J + g
                    dve.wait_ge(silu_done, 2 * u + tile + 1)
                    dve.wait_ge(gu_done, 4 * u + 2 * tile + 2)
                    nc.vector.tensor_tensor(gated[:, tile], gated[:, tile], gu_ps[:, tile, 1], ALU.mult).then_inc(mul_done, 1)
                    dve.wait_ge(a_hi_done, 2 * u + tile + 1)
                    nc.vector.tensor_tensor(a_lo[:, g, tile], gated[:, tile], a_hi[:, g, tile].bitcast(F32),
                                            ALU.subtract).then_inc(a_lo_done, 1)

                def add(J, g, fresh, chunks=range(UC)):
                    for c in chunks:
                        d = 4 * (2 * J + g) + c
                        dve.wait_ge(down_done, d + 1)
                        to = total[:, g * UC + c]
                        if fresh:
                            nc.vector.tensor_copy(to, d_ps[:, c % 2]).then_inc(added, 1)
                        else:
                            dve.wait_ge(added, d - 8 + 1 + B)
                            nc.vector.tensor_tensor(to, to, d_ps[:, c % 2], ALU.add).then_inc(added, 1)

                def mean(half, g, c):
                    dve.wait_ge(squared, (half * UG + g) * UC + c + 1)
                    nc.vector.tensor_scalar(ssq[:, c:c + 1], ssq[:, c:c + 1], 1.0 / DM, RMS_EPS, ALU.mult, ALU.add).then_inc(meaned, 1)

                def close(half, g, c):
                    n, t = (half * UG + g) * UC + c, total[:, g * UC + c]
                    dve.wait_ge(rooted, n + 1)
                    if n == 0:
                        dve.wait_ge(gain_loaded, 16)
                    nc.vector.scalar_tensor_tensor(t, t, ssq[:, c:c + 1], gain[:], ALU.mult, ALU.mult).then_inc(scaled, 1)
                    dve.wait_ge(scaled, n + 1)
                    dve.wait_ge(x1_moved[n % 2], 32 * (n // 2) + 16)
                    nc.vector.tensor_tensor(x1[:, n % 2], x1[:, n % 2], t, ALU.add).then_inc(out_done, 1)

                def finish(half, g):
                    mean(half, g, 0)
                    for c in range(UC):
                        if c + 1 < UC:
                            mean(half, g, c + 1)
                        close(half, g, c)

                for i in range(2 * TILES):
                    split_gu(0, i)

                def part(J, first, last, half):
                    for g in range(UG):
                        if g == 1:
                            split_down(J)
                        products(J, g, 0)
                        more = g == 1 and not (last and half == HALVES - 1)
                        if more:
                            split_gu(J + 1, 0)
                            split_gu(J + 1, 1)
                        products(J, g, 1)
                        if g == 0:
                            if not (first and half == 0):
                                add(J - 1, 1, J == half * PARTS + 1 if isinstance(J, int) else False)
                        else:
                            add(J, 0, first)
                        if more:
                            split_gu(J + 1, 2)
                            split_gu(J + 1, 3)
                        if first and half and g == 0:
                            finish(half - 1, 1)
                        if last and g == 1:
                            finish(half, 0)

                parts(dve, part)
                for c in range(UC + 1):
                    if c < UC:
                        add(HALVES * PARTS - 1, 1, False, (c,))
                    if c:
                        mean(HALVES - 1, 1, c - 1)
                        close(HALVES - 1, 1, c - 1)


INPUTS = ["x", "positions", "w_in", "w_out", "g_pre_mix", "g_post_mix", "g_pre_ffn", "g_post_ffn",
          "w_gate", "w_up", "w_down"]


def tensors(nc, aps, given=()):
    D = {"x": aps["in_x"][0], "positions": aps["in_positions"]}
    if "out" in aps:
        D["out"] = aps["out"][0]
    for n in ("w_in", "w_out", "w_gate", "w_up", "w_down"):
        D[n] = aps[f"in_{n}"][0]
    for n in ("g_pre_mix", "g_post_mix", "g_pre_ffn", "g_post_ffn"):
        D[n] = aps[f"in_{n}"]
    for n in aps:
        if n.startswith("const_"):
            D[n[6:]] = aps[n]
    for n, shape in (("projT", (PROJ, SEQ)), ("att_out", (3, SEQ, ATT_HEADS // 2 * AO_W)), ("x1", (SEQ, DM)), ("h_hi", (DM, SEQ)), ("h_lo", (DM, SEQ))):
        if n in aps:
            D[n] = aps[n]
        else:
            D[n] = nc.dram_tensor(n, shape, F32, kind="Internal").ap()
    for n in ("rot_hi", "rot_lo"):
        D[n] = aps[n] if n in aps else nc.dram_tensor(n, (2 * WIDTH, SEQ), F32, kind="Internal").ap()
    return D


def build(nc, aps):
    D = tensors(nc, aps)
    with ExitStack() as ctx:
        keep = {n: ctx.enter_context(nc.sbuf_tensor(n, [P, KT, SEQ], F32R)) for n in ("hT_hi", "hT_lo")}
        keep["w_raw"] = ctx.enter_context(nc.sbuf_tensor("w_raw", [P, KT, P], F32))
        normed_transpose(nc, D, keep)
        project(nc, D, keep)
    with ExitStack() as ctx:
        w_out = ctx.enter_context(nc.sbuf_tensor("w_out", [P, KT, DM], F32))
        attention(nc, D, w_out)
        mix(nc, D, w_out)
    ffn(nc, D)




def constants():
    import numpy as np

    c = {"ident": np.eye(P, dtype=np.float32)}
    a, k = np.arange(P)[:, None], np.arange(P)[None, :]
    c["mask"] = np.where(np.concatenate([k >= a, k <= a], 1), 0.0, NEG).astype(np.float32)
    f = np.float32(500000.0) ** (-np.arange(0, ROPE, 2, dtype=np.float32) / np.float32(ROPE))
    att = np.zeros((ATT_D, 2), np.float32)
    att[:ROPE, 0] = np.tile(f, 2)
    att[:ROPE, 1] = np.repeat([-1.0, 1.0], ROPE // 2)
    f = np.float32(1.0) / np.float32(10000.0) ** np.linspace(0, 1, RET_DK // 2, dtype=np.float32)
    ret = np.stack([np.tile(f, 2), np.repeat([-1.0, 1.0], RET_DK // 2)], 1).astype(np.float32)
    c["rotation"] = np.concatenate([np.tile(att, (P // ATT_D, 1)), np.tile(ret, (P // RET_DK, 1))], 1)
    log_g = np.log1p(-np.exp2(-5.0 - np.arange(RET_HEADS, dtype=np.float32))).astype(np.float32).reshape(2, 4)
    i = np.arange(P, dtype=np.float32)
    scale = RET_DK ** -0.5
    c["k_decay"] = np.repeat(np.exp(log_g[None] * (P - 1.0 - i)[:, None, None]) * scale, RET_DK, 2)
    c["q_decay"] = np.repeat(np.exp(log_g[:, :, None] * (i + 1.0)), RET_DK, 1).transpose(1, 0, 2)
    ahead = i[None, :] - i[:, None]
    c["decay"] = np.where(ahead >= 0, np.exp(log_g[:, :, None, None] * np.maximum(ahead, 0.0)), 0.0).transpose(2, 0, 1, 3) * scale
    row = np.arange(P)[:, None] // RET_DK
    c["head_rows"] = (row == np.arange(4)[None]).astype(np.float32)
    c["head_cols"] = (row == np.arange(4 * RET_DV)[None] // RET_DV).astype(np.float32)
    c["chunk_decay"] = np.repeat(np.exp(log_g * P), RET_DK, 1).T
    return {n: np.ascontiguousarray(a, dtype=np.float32) for n, a in c.items()}


def kernel(**inputs):
    import numpy as np
    import concourse.bacc as bacc
    from concourse.bass_utils import run_bass_kernel_spmd

    arrays = {f"in_{n}": np.ascontiguousarray(inputs[n]) for n in INPUTS}
    arrays.update({f"const_{n}": a for n, a in constants().items()})
    nc = bacc.Bacc("TRN2", target_bir_lowering=False, num_devices=1)
    aps = {n: nc.dram_tensor(n, a.shape, mybir.dt.from_np(a.dtype), kind="ExternalInput").ap() for n, a in arrays.items()}
    aps["out"] = nc.dram_tensor("out", (1, SEQ, DM), F32, kind="ExternalOutput").ap()
    build(nc, aps)
    r = run_bass_kernel_spmd(nc, [arrays], core_ids=[0])
    return r.results[0]["out"]
```
